# Optimizing a Trainium2 kernel written in Bass

```python
import math
import jax, jax.numpy as jnp
from jax import lax
import numpy as np

D_MODEL = 1024
BATCH = 1
SEQ = 512
DEPTH = 2

MLA_HEADS = 8
MLA_NOPE = 64
MLA_ROPE = 32
MLA_V = 64
Q_LORA = 256
KV_LORA = 256
DIFF_HEADS = 4
DIFF_D = 64
D_FF = 4 * D_MODEL

MLA_WIDTH = MLA_HEADS * MLA_V
DIFF_WIDTH = DIFF_HEADS * 2 * DIFF_D
D_MIX = MLA_WIDTH + DIFF_WIDTH

OFF_CQ = 0
OFF_CKV = OFF_CQ + Q_LORA
OFF_KR = OFF_CKV + KV_LORA
OFF_DQ = OFF_KR + MLA_ROPE
OFF_DK = OFF_DQ + DIFF_HEADS * 2 * DIFF_D
OFF_DV = OFF_DK + DIFF_HEADS * 2 * DIFF_D
P_IN = OFF_DV + DIFF_HEADS * 2 * DIFF_D

Q_BLOCK = 128
ROPE_THETA = 10000.0
EPS = 1e-6
SUBLN_EPS = 1e-5

kernel_name = "hybrid_mla_diffattn_alibi_encoder"

def _rmsnorm(x, g, eps=EPS):
    xf = x.astype(jnp.float32)
    y = xf * lax.rsqrt(jnp.mean(xf * xf, axis=-1, keepdims=True) + eps)
    return (y * g.astype(jnp.float32)).astype(x.dtype)

def _rope(x, cos, sin):
    half = x.shape[-1] // 2
    xf = x.astype(jnp.float32)
    x1, x2 = xf[..., :half], xf[..., half:]
    return jnp.concatenate([x1 * cos - x2 * sin, x1 * sin + x2 * cos], axis=-1).astype(x.dtype)

def _alibi_slopes(n_heads):
    return jnp.exp2(-8.0 * (jnp.arange(n_heads, dtype=jnp.float32) + 1.0) / n_heads)

def _to_blocks(t):
    b, s = t.shape[:2]
    t = t.reshape((b, s // Q_BLOCK, Q_BLOCK) + t.shape[2:])
    return jnp.moveaxis(t, 1, 0)

def _from_blocks(t):
    t = jnp.moveaxis(t, 0, 1)
    return t.reshape((t.shape[0], t.shape[1] * t.shape[2]) + t.shape[3:])

def _mla_attention(q, k, v):
    scale = (MLA_NOPE + MLA_ROPE) ** -0.5

    def one_block(qb):
        s = jnp.einsum('bqhd,bkhd->bhqk', qb, k, preferred_element_type=jnp.float32) * scale
        p = jax.nn.softmax(s, axis=-1).astype(v.dtype)
        return jnp.einsum('bhqk,bkhd->bqhd', p, v)

    return _from_blocks(lax.map(one_block, _to_blocks(q)))

def _diff_attention(q, k, v, lam, slopes):
    s_len = k.shape[1]
    scale = DIFF_D ** -0.5
    kpos = jnp.arange(s_len, dtype=jnp.float32)
    starts = jnp.arange(s_len // Q_BLOCK, dtype=jnp.int32) * Q_BLOCK

    def one_block(args):
        qb, start = args
        qpos = (start + jnp.arange(Q_BLOCK, dtype=jnp.int32)).astype(jnp.float32)
        bias = -slopes[:, None, None] * jnp.abs(qpos[:, None] - kpos[None, :])
        s = jnp.einsum('bqhmd,bkhmd->bmhqk', qb, k,
                       preferred_element_type=jnp.float32) * scale + bias
        p = jax.nn.softmax(s, axis=-1)
        w = (p[:, 0] - lam * p[:, 1]).astype(v.dtype)
        return jnp.einsum('bhqk,bkhd->bqhd', w, v)

    return _from_blocks(lax.map(one_block, (_to_blocks(q), starts)))

def setup_inputs(seed: int = 0) -> dict:
    key = jax.random.key(seed)
    ks = jax.random.split(key, 18)
    f32 = jnp.float32
    L = DEPTH

    def w(k, shape, fan_in):
        return jax.random.normal(k, shape, f32) * (fan_in ** -0.5)

    def gain(k, shape):
        return 1.0 + 0.01 * jax.random.normal(k, shape, f32)

    return {
        "x": jax.random.normal(ks[0], (BATCH, SEQ, D_MODEL), f32),
        "w_in": w(ks[1], (L, D_MODEL, P_IN), D_MODEL),
        "g_mix": gain(ks[2], (L, D_MODEL)),
        "g_q": gain(ks[3], (L, Q_LORA)),
        "g_kv": gain(ks[4], (L, KV_LORA)),
        "w_uq": w(ks[5], (L, Q_LORA, MLA_HEADS * (MLA_NOPE + MLA_ROPE)), Q_LORA),
        "w_ukv": w(ks[6], (L, KV_LORA, MLA_HEADS * (MLA_NOPE + MLA_V)), KV_LORA),
        "lam_q1": 0.1 * jax.random.normal(ks[7], (L, DIFF_D), f32),
        "lam_k1": 0.1 * jax.random.normal(ks[8], (L, DIFF_D), f32),
        "lam_q2": 0.1 * jax.random.normal(ks[9], (L, DIFF_D), f32),
        "lam_k2": 0.1 * jax.random.normal(ks[10], (L, DIFF_D), f32),
        "g_sub": gain(ks[11], (L, 2 * DIFF_D)),
        "w_out": w(ks[12], (L, D_MIX, D_MODEL), D_MIX),
        "g_mlp": gain(ks[13], (L, D_MODEL)),
        "w_up": w(ks[14], (L, D_MODEL, D_FF), D_MODEL),
        "w_down": w(ks[15], (L, D_FF, D_MODEL), D_FF),
        "g_final": gain(ks[16], (D_MODEL,)),
    }

def reference(x, w_in, g_mix, g_q, g_kv, w_uq, w_ukv, lam_q1, lam_k1, lam_q2, lam_k2,
              g_sub, w_out, g_mlp, w_up, w_down, g_final):
    b, s, _ = x.shape
    pos = jnp.arange(s, dtype=jnp.float32)
    inv_freq = 1.0 / (ROPE_THETA ** (jnp.arange(0, MLA_ROPE, 2, dtype=jnp.float32) / MLA_ROPE))
    ang = pos[:, None] * inv_freq[None, :]
    cos, sin = jnp.cos(ang), jnp.sin(ang)
    slopes = _alibi_slopes(DIFF_HEADS)

    h = x
    for l in range(DEPTH):
        lam_init = 0.8 - 0.6 * math.exp(-0.3 * l)
        u = _rmsnorm(h, g_mix[l])
        z = u @ w_in[l]

        c_q = _rmsnorm(z[..., OFF_CQ:OFF_CKV], g_q[l])
        c_kv = _rmsnorm(z[..., OFF_CKV:OFF_KR], g_kv[l])
        k_rope = _rope(z[..., OFF_KR:OFF_DQ], cos, sin)
        q = (c_q @ w_uq[l]).reshape(b, s, MLA_HEADS, MLA_NOPE + MLA_ROPE)
        q = jnp.concatenate(
            [q[..., :MLA_NOPE], _rope(q[..., MLA_NOPE:], cos[:, None], sin[:, None])], axis=-1)
        kv = (c_kv @ w_ukv[l]).reshape(b, s, MLA_HEADS, MLA_NOPE + MLA_V)
        k = jnp.concatenate(
            [kv[..., :MLA_NOPE],
             jnp.broadcast_to(k_rope[:, :, None, :], (b, s, MLA_HEADS, MLA_ROPE))], axis=-1)
        o_mla = _mla_attention(q, k, kv[..., MLA_NOPE:]).reshape(b, s, MLA_WIDTH)

        dq = z[..., OFF_DQ:OFF_DK].reshape(b, s, DIFF_HEADS, 2, DIFF_D)
        dk = z[..., OFF_DK:OFF_DV].reshape(b, s, DIFF_HEADS, 2, DIFF_D)
        dv = z[..., OFF_DV:P_IN].reshape(b, s, DIFF_HEADS, 2 * DIFF_D)
        lam = (jnp.exp(jnp.sum(lam_q1[l].astype(jnp.float32) * lam_k1[l].astype(jnp.float32)))
               - jnp.exp(jnp.sum(lam_q2[l].astype(jnp.float32) * lam_k2[l].astype(jnp.float32)))
               + lam_init)
        o = _diff_attention(dq, dk, dv, lam, slopes)
        o = _rmsnorm(o, g_sub[l], SUBLN_EPS) * (1.0 - lam_init)
        o_diff = o.reshape(b, s, DIFF_WIDTH)

        h = h + jnp.concatenate([o_mla, o_diff], axis=-1) @ w_out[l]

        u = _rmsnorm(h, g_mlp[l])
        h = h + jnp.square(jax.nn.relu(u @ w_up[l])) @ w_down[l]

    return _rmsnorm(h, g_final)


_drawn_inputs = setup_inputs


def setup_inputs(seed=0):
    import zlib

    import numpy as np

    out = dict(_drawn_inputs(seed))
    spreads = {}
    factors = {'g_mix': 5.301,
     'g_q': 8.0,
     'g_kv': 8.0,
     'lam_q2': 4.606,
     'g_sub': 26.975,
     'g_mlp': 5.051,
     'g_final': 32.244}
    for name, (base, spread) in spreads.items():
        noise = np.random.default_rng([zlib.crc32(name.encode()), seed]).standard_normal(out[name].shape)
        drawn = base * np.exp(spread * noise) if base else spread * noise
        out[name] = __import__('jax').numpy.asarray(drawn.astype(out[name].dtype))
    for name, factor in factors.items():
        out[name] = (out[name] * factor).astype(out[name].dtype)
    return out
```

```python
import math
from contextlib import ExitStack

import concourse.bass as bass
from concourse import mybir

F32 = mybir.dt.float32
F32R = mybir.dt.float32r
ALU = mybir.AluOpType
ACT = mybir.ActivationFunctionType
AX_X = mybir.AxisListType.X

P = 128
SEQ, D_MODEL, DEPTH = 512, 1024, 2
KD = D_MODEL // P
TT = SEQ // P
MLA_HEADS, NOPE, ROPE, MLA_V = 8, 64, 32, 64
LORA = 256
KC = LORA // P
DIFF_HEADS, DIFF_D = 4, 64
D_FF = 4 * D_MODEL
QK = NOPE + ROPE
DIFF_W = DIFF_HEADS * 2 * DIFF_D
OFF_CQ, OFF_CKV, OFF_KR = 0, LORA, 2 * LORA
OFF_DQ = OFF_KR + ROPE
OFF_DK = OFF_DQ + DIFF_W
OFF_DV = OFF_DK + DIFF_W
P_IN = OFF_DV + DIFF_W
EPS, SUBLN_EPS = 1e-6, 1e-5
ROPE_THETA = 10000.0
FC = 4
CHUNKS = D_FF // (FC * P)
BLK = 1024
NEGD = SEQ + (TT - 1) * P

C_TABQ, C_TABK, C_NEGD = 0, SEQ, 2 * SEQ
C_SIGN = C_NEGD + NEGD
C_INIT = C_SIGN + DEPTH
C_GSC = C_INIT + DEPTH
C_W = C_GSC + DEPTH

G_MIX, G_MLP = 0, DEPTH * KD
G_FINAL = 2 * DEPTH * KD
G_Q = G_FINAL + KD
G_KV = G_Q + DEPTH * KC
G_SUB = G_KV + DEPTH * KC
G_ROWS = G_SUB + DEPTH

SLOPES = [2.0 ** (-8.0 * (h + 1) / DIFF_HEADS) for h in range(DIFF_HEADS)]
DSTEPS = DIFF_HEADS * TT
MSTEPS = MLA_HEADS * TT
STEPS = DSTEPS + MSTEPS

A_USES = (["cq0", "cq1", "ckv0", "ckv1", "kr"] + [f"dk{h}" for h in range(DIFF_HEADS)]
          + [f"dq{h}" for h in range(DIFF_HEADS)])


def gen_uses(n):
    uses = []
    if n == DSTEPS - 2:
        uses += ["kp0", "q0"]
    if n == DSTEPS - 1:
        uses += ["q1"]
    if DSTEPS <= n < DSTEPS + TT:
        uses += [f"v{n - DSTEPS}"]
    h, r = divmod(n - DSTEPS - 1, TT)
    if n > DSTEPS and r == 0 and h + 2 < MLA_HEADS:
        if h % 2 == 0:
            uses += [f"kp{h // 2 + 1}"]
        uses += [f"q{h + 2}"]
    return uses


GEN_USES = [u for n in range(STEPS) for u in gen_uses(n)]
OUT_USES = [f"out{j}" for j in range(KD)]


def mlp_order():
    order = [("up", 0)]
    for c in range(CHUNKS):
        if c + 1 < CHUNKS:
            order.append(("up", c + 1))
        order.append(("down", c))
    return order


MLP_USES = [f"{kind}{c}_{i}" for kind, c in mlp_order() for i in range(FC if kind == "up" else KD)]
USES = A_USES + GEN_USES + OUT_USES + MLP_USES
USE = {u: k for k, u in enumerate(USES)}
BANK = {}
for names, banks in ((A_USES, (0, 1, 4)), (GEN_USES, (0, 1)), (OUT_USES + MLP_USES, (0, 1, 2, 3))):
    for k, u in enumerate(names):
        BANK[u] = banks[k % len(banks)]
NTH = {}
BANK_USES = [0] * 5
for u in USES:
    NTH[u] = BANK_USES[BANK[u]]
    BANK_USES[BANK[u]] += 1

MISC = ["mix_c", "mix_b", "q_c", "q_b", "kv_c", "kv_b"]
for g in range(DIFF_HEADS):
    MISC += [f"pv{g}", f"sub{g}_c", f"sub{g}_b"]
MISC += [f"pv{DIFF_HEADS + h}" for h in range(MLA_HEADS)] + ["mlp_c", "mlp_b"]
MISC_AT = {m: k for k, m in enumerate(MISC)}

BLOCKS = [(u, 0) for u in A_USES] + [("dv", b) for b in range(TT)]
BLOCKS += [("uq", 0), ("uq", 1), ("ukv", 0), ("ukv", 1)] + [(u, 0) for u in OUT_USES]
for kind, c in mlp_order():
    BLOCKS += [(f"{kind}{c}", i) for i in range(FC)]
BLOCK_AT = {b: k for k, b in enumerate(BLOCKS)}
NBLK = len(BLOCKS)
RING = 4


SKIP_AT = BLOCK_AT[("out0", 0)]
SLOT = [(b if b < SKIP_AT else b - SKIP_AT) % RING for b in range(NBLK)]
assert (NBLK - SKIP_AT) % RING == 0


def previous(b):
    before = [a for a in range(b) if SLOT[a] == SLOT[b]]
    if before:
        return before[-1]
    return max(a for a in range(NBLK) if SLOT[a] == SLOT[b]) - NBLK


CHAIN = 51

def trunk(nc, x, w_in, g_mix, g_q, g_kv, w_uq, w_ukv, lam_q1, lam_k1, lam_q2, lam_k2,
          g_sub, w_out, g_mlp, w_up, w_down, g_final, cst, out):
    at_byte = [16512]

    def place(name, shape, dt, at=None):
        size = 4 * int(math.prod(shape[1:]))
        if at is None:
            at = at_byte[0]
            at_byte[0] += -(-size // 32) * 32
        return nc.alloc_sbuf_tensor_at(name, shape, dt, offset=at)

    h = place("h", [P, KD, SEQ], F32)
    u_hi = place("u_hi", [P, KD, SEQ], F32R)
    u_lo = place("u_lo", [P, KD, SEQ], F32R)
    region = at_byte[0]
    dq_hi = place("dq_hi", [P, DIFF_HEADS, SEQ], F32R)
    dq_lo = place("dq_lo", [P, DIFF_HEADS, SEQ], F32R)
    dk_hi = place("dk_hi", [P, DIFF_HEADS, SEQ], F32R)
    dk_lo = place("dk_lo", [P, DIFF_HEADS, SEQ], F32R)
    dv_hi = place("dv_hi", [P, TT, SEQ], F32R)
    dv_lo = place("dv_lo", [P, TT, SEQ], F32R)
    kb = 1024
    v_pack = place("v_pack", [P, TT, MLA_HEADS, 2, MLA_V], F32R, region)
    q_hi = place("q_hi", [P, 2, SEQ], F32R, region + 16 * kb)
    q_lo = place("q_lo", [P, 2, SEQ], F32R, region + 20 * kb)
    k_pack = place("k_pack", [P, 4, 2, SEQ], F32R, region + 24 * kb)
    hid_hi = place("hid_hi", [P, 2, FC, SEQ], F32R, region + 16 * kb)
    hid_lo = place("hid_lo", [P, 2, FC, SEQ], F32R, region + 32 * kb)
    xin = place("xin", [P, TT, D_MODEL], F32, region)
    yout = place("yout", [P, TT, D_MODEL], F32, region + 32 * kb)
    c_hi = place("c_hi", [P, 2 * KC, SEQ], F32R)
    c_lo = place("c_lo", [P, 2 * KC, SEQ], F32R)
    stage = place("stage", [P, RING, BLK], F32)
    w_hi = place("w_hi", [P, RING, BLK], F32R)
    w_lo = place("w_lo", [P, RING, BLK], F32R)
    pt_hi = place("pt_hi", [P, TT, SEQ], F32R)
    pt_lo = place("pt_lo", [P, TT, SEQ], F32R)
    scratch = at_byte[0] - 16 * kb
    ss = place("ss", [P, SEQ], F32, scratch)
    rb_c = place("rb_c", [P, SEQ], F32, scratch + 2 * kb)
    ck = place("ck", [P, SEQ], F32, scratch + 4 * kb)
    e_t = place("e_t", [P, 4, SEQ], F32)
    tmp_s = place("tmp_s", [P, 2, SEQ], F32)
    tmp_y = place("tmp_y", [P, 2, SEQ], F32)
    rb = place("rb", [P, SEQ], F32)
    krf = place("krf", [P, SEQ], F32)
    consts = place("consts", [P, C_W], F32)
    ident = place("ident", [P, P], F32)
    ones = place("ones", [P, P], F32)
    diag = place("diag", [P, TT, P], F32)
    mhalf = place("mhalf", [P, TT], F32)
    rc = place("rc", [P, TT], F32)
    rs = place("rs", [P, TT], F32)
    rs_mix = place("rs_mix", [P, TT], F32)
    g_rows = place("g_rows", [P, P], F32, region + 16 * kb)
    g_cols = place("g_cols", [P, G_ROWS], F32)
    gsl = place("gsl", [P, DEPTH], F32)
    lam_r = place("lam_r", [4, 2, DIFF_D], F32, region + 17 * kb)
    lam_s = place("lam_s", [4, 4], F32)
    lam_b = place("lam_b", [P, DEPTH], F32)
    nmx = place("nmx", [P, 4], F32)
    rsum = place("rsum", [P, 4], F32)
    coefs = place("coefs", [P, 4], F32)

    tabq = consts[:, C_TABQ:C_TABQ + SEQ]
    tabk = consts[:, C_TABK:C_TABK + SEQ]
    sign = consts[0:4, C_SIGN:C_SIGN + DEPTH]

    with ExitStack() as ctx:
        bank = [ctx.enter_context(nc.psum_tensor(f"bank{b}", [P, SEQ], F32)) for b in range(8)]
        MISC_BANK, SC_BANKS, TR_BANKS, DV_BANKS = bank[5], bank[2:5], bank[6:8], [bank[2], bank[3], bank[6], bank[7]]
        per_layer, counters = {}, []

        def counter(name, per):
            sem = ctx.enter_context(nc.semaphore(name))
            per_layer[id(sem)] = per
            counters.append(sem)
            return sem

        def once(name):
            return ctx.enter_context(nc.semaphore(name))

        stage_full = [once(f"stage_full{s}") for s in range(RING)]
        w_hi_made, w_lo_made = counter("w_hi_made", NBLK), counter("w_lo_made", NBLK)
        proj_done = counter("proj_done", len(USES))
        bank_free = [counter(f"bank{b}_free", BANK_USES[b]) for b in range(5)]
        misc_done, misc_free = counter("misc_done", len(MISC)), counter("misc_free", len(MISC))
        u_hi_made, u_lo_made = counter("u_hi_made", 2 * KD), counter("u_lo_made", 2 * KD)
        sq_ready, ss_acc = counter("sq_ready", 2 * KD + 2 * KC), counter("ss_acc", 2 * KD + 2 * KC)
        pow_done, diag_ready = counter("pow_done", 4 + DIFF_HEADS), counter("diag_ready", 4 + DIFF_HEADS)
        c_ready, c_hi_made, c_lo_made = (counter(n, 2 * KC) for n in ("c_ready", "c_hi_made", "c_lo_made"))
        kr_half, kr_ready = counter("kr_half", 1), counter("kr_ready", 1)
        krb_hi_made, krb_lo_made = counter("krb_hi_made", 4), counter("krb_lo_made", 4)
        d_hi_made, d_lo_made = counter("d_hi_made", 2 * DIFF_HEADS), counter("d_lo_made", 2 * DIFF_HEADS)
        dv_done, dv_hi_made, dv_lo_made = (counter(n, TT) for n in ("dv_done", "dv_hi_made", "dv_lo_made"))
        v_hi_made, k_hi_made = counter("v_hi_made", TT), counter("k_hi_made", MLA_HEADS)
        qf_ready, q_hi_made, q_lo_made = (counter(n, MLA_HEADS) for n in ("qf_ready", "q_hi_made", "q_lo_made"))
        sc_done, sc_free = (counter(n, 2 * DSTEPS + MSTEPS) for n in ("sc_done", "sc_free"))
        mx_ready, e_ready = counter("mx_ready", MSTEPS), counter("e_ready", 2 * DSTEPS)
        coef_ready, t1_ready, w_ready = counter("coef_ready", DSTEPS), counter("t1_ready", DSTEPS), counter("w_ready", STEPS)
        tr_done, pt_hi_made, pt_lo_made = (counter(n, STEPS) for n in ("tr_done", "pt_hi_made", "pt_lo_made"))
        o_half = counter("o_half", MLA_HEADS)
        o_hi_made, o_lo_made = counter("o_hi_made", KD), counter("o_lo_made", KD)
        hid_f, hid_hi_made, hid_lo_made = (counter(n, CHUNKS * FC) for n in ("hid_f", "hid_hi_made", "hid_lo_made"))
        chain_done = counter("chain_done", CHAIN)
        c_in, x_in, g_in, consts_made = once("c_in"), once("x_in"), once("g_in"), once("consts_made")
        xt_done, gt_done, gt_copied = once("xt_done"), once("gt_done"), once("gt_copied")
        lam_e, lam_m, lam_done = once("lam_e"), once("lam_m"), once("lam_done")
        y_ready, yt_done, y_copied, y_out = once("y_ready"), once("yt_done"), once("y_copied"), once("y_out")

        def val(sem, l, k):
            return (l + 1) * per_layer[id(sem)] + k

        def freed(use):
            return bank_free[BANK[use]]

        def read_out(l, use):
            return freed(use), val(freed(use), l, NTH[use] + 1)

        def taken(l, use):
            return freed(use), val(freed(use), l, NTH[use])

        def stream_ready(l, j):
            return read_out(l - 1, f"down{CHUNKS - 1}_{j}")

        def block_used(l, b):
            if b < 0:
                l, b = l - 1, b + NBLK
            name, i = BLOCKS[b]
            if name == "dv":
                return dv_done, val(dv_done, l, i + 1)
            use = name
            if name in ("uq", "ukv"):
                use = GEN_USES[-1]
            elif name.startswith("up"):
                use = f"{name}_{i}"
            elif name.startswith("down"):
                use = f"{name}_{2 * i + 1}"
            return proj_done, val(proj_done, l, USE[use] + 1)

        def staged(l, b):
            s = SLOT[b]
            return stage_full[s], (l * SLOT.count(s) + SLOT[:b].count(s) + 1) * 16

        def layers(eng):
            return range(DEPTH)

        def cols(tile, base, l, per=1):
            return tile[:, bass.ds(l * per + base, 1)]

        def block_parts(b):
            name, _ = BLOCKS[b]
            if name == "kr":
                hi = lambda t, s: t[:, s, :].rearrange("p (k c) -> p k c", k=KD)
                st = lambda s: stage[:, s, 0:KD * ROPE].rearrange("p (k c) -> p k c", k=KD)
                half = ROPE // 2
                return hi, st, [(0, 0, ROPE), (ROPE, half, half), (ROPE + half, 0, half)]
            if name == "uq":
                hi = lambda t, s: t[:, s, :].rearrange("p (h c) -> p h c", h=MLA_HEADS)
                st = lambda s: stage[:, s, 0:MLA_HEADS * QK].rearrange("p (h c) -> p h c", h=MLA_HEADS)
                half = ROPE // 2
                return hi, st, [(0, 0, QK), (QK, NOPE + half, half), (QK + half, NOPE, half)]
            if name == "ukv":
                hi = lambda t, s: t[:, s, :].rearrange("p (a h c) -> p h a c", a=2, h=MLA_HEADS)
                st = lambda s: stage[:, s, :].rearrange("p (h a c) -> p h a c", a=2, h=MLA_HEADS)
                return hi, st, [(0, 0, 2)]
            hi = lambda t, s: t[:, s:s + 1, :]
            st = lambda s: stage[:, s:s + 1, :]
            return hi, st, [(0, 0, BLK)]

        block = ctx.enter_context(nc.Block())

        @block.sync
        def _(sp):
            for sem in counters:
                sp.sem_inc(sem, per_layer[id(sem)] - (2 if any(sem is f for f in bank_free[0:4]) else 0))
            for j in range(2):
                sp.dma_start(xin[:, :, j * SEQ:(j + 1) * SEQ],
                             x[0].rearrange("(t p) d -> p t d", p=P)[:, :, j * SEQ:(j + 1) * SEQ]).then_inc(x_in, 16)
            for l in layers(sp):
                for b, (name, i) in enumerate(BLOCKS):
                    s = SLOT[b]
                    sp.wait_ge(w_hi_made, val(w_hi_made, l, previous(b) + 1))
                    sp.wait_ge(w_lo_made, val(w_lo_made, l, previous(b) + 1))
                    dst = stage[:, s, :]
                    if name == "dv":
                        src = w_in[l].rearrange("(k p) m -> p k m", p=P)[:, 2 * i:2 * i + 2, OFF_DV:P_IN]
                        dst = dst.rearrange("p (k m) -> p k m", k=2)
                    elif name == "uq":
                        src = w_uq[l][i * P:(i + 1) * P, :]
                        dst = stage[:, s, 0:MLA_HEADS * QK]
                    elif name == "ukv":
                        src = w_ukv[l][i * P:(i + 1) * P, :]
                    elif name == "kr":
                        src = w_in[l].rearrange("(k p) m -> p k m", p=P)[:, :, OFF_KR:OFF_DQ]
                        dst = stage[:, s, 0:KD * ROPE].rearrange("p (k m) -> p k m", k=KD)
                    elif name.startswith("down"):
                        c = int(name[4:])
                        src = w_down[l].rearrange("(k p) m -> p k m", p=P)[:, c * FC:(c + 1) * FC, i * 256:(i + 1) * 256]
                        dst = dst.rearrange("p (k m) -> p k m", k=FC)
                    else:
                        if name.startswith("up"):
                            w, c0 = w_up, (int(name[2:]) * FC + i) * P
                        elif name.startswith("out"):
                            w, c0 = w_out, int(name[3:]) * P
                        else:
                            base = {"cq": OFF_CQ, "ckv": OFF_CKV, "dk": OFF_DK, "dq": OFF_DQ}[name[:-1]]
                            w, c0 = w_in, base + int(name[-1]) * P
                        src = w[l].rearrange("(k p) m -> p k m", p=P)[:, :, c0:c0 + P]
                        dst = dst.rearrange("p (k m) -> p k m", k=KD)
                    sp.dma_start(dst, src).then_inc(stage_full[s], 16)
            sp.wait_ge(y_copied, KD)
            sp.dma_start(out[0].rearrange("(t p) d -> p t d", p=P), yout[:, :, :]).then_inc(y_out, 16)
            sp.wait_ge(y_out, 16)

        @block.gpsimd
        def _(pool):
            nc.gpsimd.memset(ident[:, :], 0.0).then_inc(consts_made, 1)
            nc.gpsimd.memset(ones[:, :], 1.0).then_inc(consts_made, 1)
            nc.gpsimd.memset(mhalf[:, :], -0.5).then_inc(consts_made, 1)
            pool.wait_ge(consts_made, 3)
            nc.gpsimd.affine_select(out=ident[:, :], in_=ident[:, :], compare_op=ALU.not_equal, fill=1.0,
                                    base=0, pattern=[[-1, P]], channel_multiplier=1).then_inc(consts_made, 1)

            def power(l, m, k, dst):
                pool.wait_ge(misc_free, val(misc_free, l, m + 1))
                nc.gpsimd.tensor_tensor(dst[:, :], rc[:, :], mhalf[:, :], ALU.pow).then_inc(pow_done, 1)

            for l in layers(pool):
                power(l, MISC_AT["mix_c"], 0, rs_mix)
                power(l, MISC_AT["q_c"], 1, rs)
                power(l, MISC_AT["kv_c"], 2, rs)
                for g in range(DIFF_HEADS):
                    power(l, MISC_AT[f"sub{g}_c"], 3 + g, rs)
                power(l, MISC_AT["mlp_c"], 3 + DIFF_HEADS, rs)
            power(DEPTH, 0, 0, rs)

        @block.scalar
        def _(act):
            act.dma_start(consts[:, :], cst).then_inc(c_in, 16)
            for w, r0, n in ((g_mix, G_MIX, DEPTH * KD), (g_mlp, G_MLP, DEPTH * KD), (g_q, G_Q, DEPTH * KC),
                             (g_kv, G_KV, DEPTH * KC), (g_sub, G_SUB, DEPTH)):
                act.dma_start(g_rows[r0:r0 + n, :], w.rearrange("l (t p) -> (l t) p", p=P)).then_inc(g_in, 16)
            act.dma_start(g_rows[G_FINAL:G_FINAL + KD, :], g_final.rearrange("(t p) -> t p", p=P)).then_inc(g_in, 16)
            for side, (a, b) in enumerate(((lam_q1, lam_q2), (lam_k1, lam_k2))):
                act.dma_start(lam_r[0:2, side, :], a).then_inc(g_in, 16)
                act.dma_start(lam_r[2:4, side, :], b).then_inc(g_in, 16)
            act.wait_ge(lam_e, 1)
            nc.scalar.activation(lam_s[:, 1:2], lam_s[:, 0:1], ACT.Exp).then_inc(lam_e, 1)

            def split(l, b):
                s = SLOT[b]
                act.wait_ge(*staged(l, b))
                act.wait_ge(*block_used(l, previous(b)))
                hi, st, parts = block_parts(b)
                for d, f, n in parts:
                    last = nc.scalar.activation(hi(w_hi, s)[:, :, d:d + n], st(s)[:, :, f:f + n], ACT.Copy)
                last.then_inc(w_hi_made, 1)

            def square(l, n, src):
                act.wait_ge(ss_acc, val(ss_acc, l, n - 1))
                nc.scalar.activation(tmp_s[:, n % 2, :], src, ACT.Square).then_inc(sq_ready, 1)

            def exp_diff(l, e, i):
                act.wait_ge(sc_free, val(sc_free, l, e + 1))
                nc.scalar.activation(e_t[:, e % 4, :], e_t[:, e % 4, :], ACT.Exp, scale=-1.0, bias=nmx[:, e % 4:e % 4 + 1],
                                     accum_out=rsum[:, e % 4:e % 4 + 1]).then_inc(e_ready, 1)

            def t1(l, i):
                act.wait_ge(coef_ready, val(coef_ready, l, i + 1))
                t = 2 * (i % 2) + 1
                nc.scalar.activation(e_t[:, t, :], e_t[:, t, :], ACT.Copy, scale=coefs[:, t:t + 1]).then_inc(t1_ready, 1)

            def exp_mla(l, i):
                act.wait_ge(mx_ready, val(mx_ready, l, i + 1))
                act.wait_ge(tr_done, val(tr_done, l, DSTEPS + i - 3))
                if i < 4:
                    act.wait_ge(tr_done, val(tr_done, l, DSTEPS))
                e = 2 * DSTEPS + i
                nc.scalar.activation(e_t[:, i % 4, :], SC_BANKS[e % 3][:, :], ACT.Exp, bias=nmx[:, i % 4:i % 4 + 1],
                                     accum_out=rsum[:, i % 4:i % 4 + 1]).then_inc(sc_free, 1)

            def hi_pt(l, n):
                act.wait_ge(tr_done, val(tr_done, l, n + 1))
                if n % TT == 0:
                    g = n // TT
                    act.wait_ge(misc_done, val(misc_done, l, MISC_AT[f"pv{g - 1}"] + 1 if g else 0))
                q = n % TT
                nc.scalar.activation(pt_hi[:, :, q * P:(q + 1) * P], TR_BANKS[n % 2].rearrange("p (k c) -> p k c", k=TT),
                                     ACT.Copy).then_inc(pt_hi_made, 1)

            def gen(l, use):
                if use[0] == "v":
                    tt = int(use[1:])
                    act.wait_ge(proj_done, val(proj_done, l, USE[use] + 1))
                    nc.scalar.activation(v_pack[:, tt, :, 0, :], bank[BANK[use]].rearrange("p (h c) -> p h c", h=MLA_HEADS),
                                         ACT.Copy).then_inc(v_hi_made, 1)
                elif use[0] == "k":
                    j = int(use[2:])
                    act.wait_ge(proj_done, val(proj_done, l, USE[use] + 1))
                    act.wait_ge(sc_done, val(sc_done, l, 2 * DSTEPS + max(0, TT * (2 * j - 2))))
                    if j == 1:
                        act.wait_ge(misc_done, val(misc_done, l, MISC_AT[f"pv{DIFF_HEADS - 1}"] + 1))
                    for p in range(2):
                        nc.scalar.activation(k_pack[0:NOPE, 2 * (j % 2) + p, 0, :],
                                             bank[BANK[use]][p * NOPE:(p + 1) * NOPE, :], ACT.Copy
                                             ).then_inc(k_hi_made, 1)
                else:
                    hd = int(use[1:])
                    act.wait_ge(qf_ready, val(qf_ready, l, hd + 1))
                    act.wait_ge(sc_done, val(sc_done, l, 2 * DSTEPS + max(0, TT * (hd - 1))))
                    nc.scalar.activation(q_hi[0:QK, hd % 2, :], tmp_y[0:QK, 0, :], ACT.Copy).then_inc(q_hi_made, 1)

            def pv_out(l, g):
                act.wait_ge(misc_done, val(misc_done, l, MISC_AT[f"pv{g}"] + 1))
                if g < DIFF_HEADS:
                    act.wait_ge(o_lo_made, val(o_lo_made, l, g))
                    nc.scalar.activation(tmp_s[:, 0, :], MISC_BANK[:, :], ACT.Copy)
                    nc.scalar.activation(tmp_s[:, 1, :], MISC_BANK[:, :], ACT.Square).then_inc(misc_free, 1)
                else:
                    act.wait_ge(misc_free, val(misc_free, l, MISC_AT[f"pv{g}"]))
                    nc.scalar.activation(tmp_s[0:MLA_V, 1, :], MISC_BANK[MLA_V:P, :], ACT.Copy).then_inc(o_half, 1)

            def o_split(l, n, t):
                if n < DIFF_HEADS:
                    act.wait_ge(misc_free, val(misc_free, l, MISC_AT[f"sub{n}_b"] + 1))
                else:
                    act.wait_ge(misc_free, val(misc_free, l, MISC_AT[f"pv{2 * n - DIFF_HEADS + 1}"] + 1))
                nc.scalar.activation(u_hi[:, t, :], tmp_s[:, 0, :], ACT.Copy).then_inc(o_hi_made, 1)

            for b in range(RING):
                split(0, b)
            act.wait_ge(gt_copied, 1)
            for l in layers(act):
                for j in range(KD):
                    act.wait_ge(*stream_ready(l, j))
                    if j == 0:
                        act.wait_ge(proj_done, val(proj_done, l - 1, USE[f"up{CHUNKS - 1}_{FC - 1}"] + 1))
                    nc.scalar.activation(u_hi[:, j, :], h[:, j, :], ACT.Copy, scale=cols(g_cols, G_MIX + j, l, KD)
                                         ).then_inc(u_hi_made, 1)
                    square(l, j, h[:, j, :])
                for k, use in enumerate(A_USES):
                    split(l, k + RING)
                    if use in ("cq0", "cq1", "ckv0", "ckv1"):
                        act.wait_ge(*read_out(l, use))
                        square(l, KD + k, e_t[:, k, :])
                    if use == "kr":
                        act.wait_ge(proj_done, val(proj_done, l, USE[use] + 1))
                        nc.scalar.activation(krf[0:2 * ROPE, :], bank[BANK[use]][2 * ROPE:4 * ROPE, :], ACT.Copy
                                             ).then_inc(kr_half, 1)
                    if use[0] == "d":
                        i = A_USES.index(use) - 5
                        act.wait_ge(*read_out(l, use))
                        dst = (dk_hi if i < DIFF_HEADS else dq_hi)[:, i % DIFF_HEADS, :]
                        nc.scalar.activation(dst, tmp_y[:, i % 2, :], ACT.Copy).then_inc(d_hi_made, 1)
                    if use in ("dk2", "dk3"):
                        for i in (0, 1) if use == "dk2" else (2, 3):
                            act.wait_ge(c_ready, val(c_ready, l, i + 1))
                            nc.scalar.activation(c_hi[:, i, :], e_t[:, i, :], ACT.Copy).then_inc(c_hi_made, 1)
                for b in range(TT):
                    split(l, BLOCK_AT[("dv", b)] + RING)
                for tt in range(TT):
                    act.wait_ge(dv_done, val(dv_done, l, TT))
                    nc.scalar.activation(dv_hi[:, tt, :], DV_BANKS[tt][:, :], ACT.Copy, scale=rs_mix[:, tt:tt + 1]
                                         ).then_inc(dv_hi_made, 1)
                for n in range(STEPS + 3):
                    if n < DSTEPS + 1 and n:
                        t1(l, n - 1)
                    if 2 <= n < STEPS + 2:
                        hi_pt(l, n - 2)
                    if n < DSTEPS:
                        exp_diff(l, 2 * n, n)
                        exp_diff(l, 2 * n + 1, n)
                    elif n < STEPS:
                        exp_mla(l, n - DSTEPS)
                    if n in (DSTEPS - 1, DSTEPS + 2):
                        for p in (0, 1) if n == DSTEPS - 1 else (2, 3):
                            act.wait_ge(kr_ready, val(kr_ready, l, 1))
                            act.wait_ge(sc_done, val(sc_done, l, 2 * DSTEPS))
                            if p >= 2:
                                act.wait_ge(misc_done, val(misc_done, l, MISC_AT[f"pv{DIFF_HEADS - 1}"] + 1))
                            nc.scalar.activation(k_pack[NOPE:QK, p, 0, :], krf[NOPE:QK, :], ACT.Copy
                                                 ).then_inc(krb_hi_made, 1)
                    for use in step_gens(n):
                        gen(l, use)
                    g, r = divmod(n - 5, TT)
                    if r == 0 and 0 <= g < DIFF_HEADS + MLA_HEADS:
                        pv_out(l, g)
                    if r == 3 and 0 <= g < DIFF_HEADS:
                        o_split(l, g, DIFF_HEADS + g)
                    if r == 2 and g >= DIFF_HEADS and (g - DIFF_HEADS) % 2 == 1:
                        hd = g - DIFF_HEADS
                        if hd < MLA_HEADS:
                            o_split(l, DIFF_HEADS + hd // 2, hd // 2)
                    if n in OUT_SPLITS:
                        split(l, OUT_SPLITS[n])
                o_split(l, KD - 1, MLA_HEADS // 2 - 1)
                for j in range(KD):
                    split(l, BLOCK_AT[(f"out{j}", 0)] + RING)
                    act.wait_ge(*read_out(l, f"out{j}"))
                    square(l, KD + 2 * KC + j, h[:, j, :])
                for j in range(KD):
                    act.wait_ge(proj_done, val(proj_done, l, USE["out7"] + 1))
                    nc.scalar.activation(u_hi[:, j, :], h[:, j, :], ACT.Copy, scale=cols(g_cols, G_MLP + j, l, KD)
                                         ).then_inc(u_hi_made, 1)
                b = BLOCK_AT[("up0", 0)]
                f = 0
                for kind, c in mlp_order():
                    for i in range(FC):
                        if b + RING < NBLK:
                            split(l, b + RING)
                        elif l + 1 < DEPTH:
                            split(l + 1, b + RING - NBLK)
                        b += 1
                        if kind == "up":
                            act.wait_ge(hid_f, val(hid_f, l, f + 1))
                            if i == 0:
                                if c >= 2:
                                    act.wait_ge(proj_done, val(proj_done, l, USE[f"down{c - 2}_{KD - 1}"] + 1))
                            nc.scalar.activation(hid_hi[:, c % 2, i, :], tmp_y[:, 1, :], ACT.Copy).then_inc(hid_hi_made, 1)
                            f += 1
            for j in range(KD):
                act.wait_ge(*stream_ready(DEPTH, j))
                square(DEPTH, j, h[:, j, :])

        @block.vector
        def _(dve):
            chain = [0]

            def link(l, ins):
                chain[0] += 1
                ins.then_inc(chain_done, 1)
                dve.wait_ge(chain_done, val(chain_done, l, chain[0]))

            def split(l, b):
                s = SLOT[b]
                dve.wait_ge(w_hi_made, val(w_hi_made, l, b + 1))
                if BLOCKS[b][0] == "kr":
                    dve.wait_ge(*block_used(l, previous(b)))
                hi, st, parts = block_parts(b)
                for d, f, n in parts:
                    dst = (hi(w_hi, s)[:, :, 2 * ROPE + d:2 * ROPE + d + n] if BLOCKS[b][0] == "kr"
                           else hi(w_lo, s)[:, :, d:d + n])
                    last = nc.vector.tensor_tensor(dst, st(s)[:, :, f:f + n],
                                                   hi(w_hi, s)[:, :, d:d + n].bitcast(F32), ALU.subtract)
                last.then_inc(w_lo_made, 1)

            def add_square(l, n, first):
                dve.wait_ge(sq_ready, val(sq_ready, l, n + 1))
                if first:
                    nc.vector.tensor_copy(ss[:, :], tmp_s[:, n % 2, :]).then_inc(ss_acc, 1)
                else:
                    dve.wait_ge(ss_acc, val(ss_acc, l, n))
                    nc.vector.tensor_tensor(ss[:, :], ss[:, :], tmp_s[:, n % 2, :], ALU.add).then_inc(ss_acc, 1)

            def stat_col(l, m, count, eps):
                dve.wait_ge(misc_done, val(misc_done, l, m + 1))
                nc.vector.tensor_scalar(rc[:, :], MISC_BANK[:, 0:TT], 1.0 / count, eps, ALU.mult, ALU.add
                                        ).then_inc(misc_free, 1)

            def stat_diag(l, k, src):
                dve.wait_ge(pow_done, val(pow_done, l, k + 1))
                for tt in range(TT):
                    last = nc.vector.tensor_scalar(diag[:, tt, :], ident[:, :], src[:, tt:tt + 1], None, ALU.mult)
                last.then_inc(diag_ready, 1)

            def stat_row(l, m, dst):
                dve.wait_ge(misc_done, val(misc_done, l, m + 1))
                nc.vector.tensor_copy(dst, MISC_BANK[:, :]).then_inc(misc_free, 1)
                dve.wait_ge(misc_free, val(misc_free, l, m + 1))

            def ttr(l, e):
                i, m = divmod(e, 2)
                hd, qt = divmod(i, TT)
                dve.wait_ge(sc_done, val(sc_done, l, e + 1))
                dve.wait_ge(tr_done, val(tr_done, l, i - 1 if i >= 2 else 0))
                off = C_NEGD + (TT - 1 - qt) * P
                nc.vector.tensor_tensor_reduce(e_t[:, e % 4, :], SC_BANKS[e % 3][:, :], consts[:, off:off + SEQ],
                                               -SLOPES[hd], 3.0e38, ALU.add, ALU.min, nmx[:, e % 4:e % 4 + 1]
                                               ).then_inc(sc_free, 1)

            def coef(l, i):
                t = 2 * (i % 2)
                dve.wait_ge(e_ready, val(e_ready, l, 2 * i + 2))
                link(l, nc.vector.reciprocal(coefs[:, t:t + 2], rsum[:, t:t + 2]))
                nc.vector.tensor_scalar(coefs[:, t + 1:t + 2], coefs[:, t + 1:t + 2], cols(lam_b, 0, l), None, ALU.mult
                                        ).then_inc(coef_ready, 1)

            def weights(l, i):
                t = 2 * (i % 2)
                dve.wait_ge(t1_ready, val(t1_ready, l, i + 1))
                nc.vector.scalar_tensor_tensor(out=e_t[:, t, :], in0=e_t[:, t, :], scalar=coefs[:, t:t + 1],
                                               in1=e_t[:, t + 1, :], op0=ALU.mult, op1=ALU.subtract
                                               ).then_inc(w_ready, 1)

            def row_max(l, i):
                e = 2 * DSTEPS + i
                dve.wait_ge(sc_done, val(sc_done, l, e + 1))
                nc.vector.tensor_reduce(nmx[:, i % 4:i % 4 + 1], SC_BANKS[e % 3][:, :], AX_X, ALU.max, negate=True
                                        ).then_inc(mx_ready, 1)

            def normalise(l, i):
                dve.wait_ge(sc_free, val(sc_free, l, 2 * DSTEPS + i + 1))
                link(l, nc.vector.reciprocal(coefs[:, i % 4:i % 4 + 1], rsum[:, i % 4:i % 4 + 1]))
                nc.vector.tensor_scalar(e_t[:, i % 4, :], e_t[:, i % 4, :], coefs[:, i % 4:i % 4 + 1], None, ALU.mult
                                        ).then_inc(w_ready, 1)

            def lo_pt(l, n):
                q = n % TT
                dve.wait_ge(pt_hi_made, val(pt_hi_made, l, n + 1))
                piece = lambda t: t[:, :, q * P:(q + 1) * P]
                nc.vector.tensor_tensor(piece(pt_lo), TR_BANKS[n % 2].rearrange("p (k c) -> p k c", k=TT),
                                        piece(pt_hi).bitcast(F32), ALU.subtract).then_inc(pt_lo_made, 1)

            def gen(l, use):
                b = bank[BANK[use]]
                dve.wait_ge(proj_done, val(proj_done, l, USE[use] + 1))
                if use[0] == "v":
                    tt = int(use[1:])
                    dve.wait_ge(v_hi_made, val(v_hi_made, l, tt + 1))
                    nc.vector.tensor_tensor(v_pack[:, tt, :, 1, :], b.rearrange("p (h c) -> p h c", h=MLA_HEADS),
                                            v_pack[:, tt, :, 0, :].bitcast(F32), ALU.subtract).then_inc(freed(use), 1)
                elif use[0] == "k":
                    j = int(use[2:])
                    for p in range(2):
                        dve.wait_ge(k_hi_made, val(k_hi_made, l, 2 * j + p + 1))
                        s = 2 * (j % 2) + p
                        last = nc.vector.tensor_tensor(k_pack[0:NOPE, s, 1, :], b[p * NOPE:(p + 1) * NOPE, :],
                                                       k_pack[0:NOPE, s, 0, :].bitcast(F32), ALU.subtract)
                    last.then_inc(freed(use), 1)
                else:
                    hd = int(use[1:])
                    nc.vector.tensor_tensor(tmp_y[0:QK, 0, :], b[0:QK, :], tabq[0:QK, :], ALU.mult)
                    nc.vector.tensor_tensor(tmp_y[NOPE:QK, 1, :], b[QK:P, :], tabq[QK:P, :], ALU.mult
                                            ).then_inc(freed(use), 1)
                    dve.wait_ge(*read_out(l, use))
                    nc.vector.tensor_tensor(tmp_y[NOPE:QK, 0, :], tmp_y[NOPE:QK, 0, :], tmp_y[NOPE:QK, 1, :], ALU.add
                                            ).then_inc(qf_ready, 1)

            def gen_q_low(l, hd):
                dve.wait_ge(q_hi_made, val(q_hi_made, l, hd + 1))
                nc.vector.tensor_tensor(q_lo[0:QK, hd % 2, :], tmp_y[0:QK, 0, :], q_hi[0:QK, hd % 2, :].bitcast(F32),
                                        ALU.subtract).then_inc(q_lo_made, 1)

            def o_low(l, n, t):
                dve.wait_ge(o_hi_made, val(o_hi_made, l, n + 1))
                nc.vector.tensor_tensor(u_lo[:, t, :], tmp_s[:, 0, :], u_hi[:, t, :].bitcast(F32), ALU.subtract
                                        ).then_inc(o_lo_made, 1)

            def pv_out(l, g):
                hd = g - DIFF_HEADS
                p = (hd % 2) * MLA_V
                dve.wait_ge(o_half, val(o_half, l, hd + 1))
                nc.vector.tensor_tensor(tmp_s[p:p + MLA_V, 0, :], MISC_BANK[0:MLA_V, :], tmp_s[0:MLA_V, 1, :], ALU.add
                                        ).then_inc(misc_free, 1)

            for j in range(KD):
                dve.wait_ge(xt_done, j + 1)
                nc.vector.tensor_copy(h[:, j, :], bank[j % 4][:, :]).then_inc(bank_free[j % 4], 1)
                if j == 0:
                    dve.wait_ge(gt_done, 1)
                    nc.vector.tensor_copy(g_cols[:, :], bank[6][:, 0:G_ROWS]).then_inc(gt_copied, 1)
            dve.wait_ge(g_in, 160)
            nc.vector.tensor_tensor_reduce(lam_r[:, 0, :], lam_r[:, 0, :], lam_r[:, 1, :], 1.0, 0.0, ALU.mult, ALU.add,
                                           lam_s[:, 0:1]).then_inc(lam_e, 1)
            for b in range(RING):
                split(0, b)
            dve.wait_ge(c_in, 16)
            dve.wait_ge(lam_e, 2)
            nc.vector.tensor_scalar(lam_s[:, 2:2 + DEPTH], sign, lam_s[:, 1:2], None, ALU.mult).then_inc(lam_m, 1)
            dve.wait_ge(lam_m, 2)
            nc.vector.tensor_tensor(lam_b[:, :], bank[7][:, 0:DEPTH], consts[:, C_INIT:C_INIT + DEPTH], ALU.add
                                    ).then_inc(lam_done, 1)
            nc.vector.tensor_tensor(gsl[:, :], g_cols[:, G_SUB:G_SUB + DEPTH], consts[:, C_GSC:C_GSC + DEPTH], ALU.mult
                                    ).then_inc(lam_done, 1)
            dve.wait_ge(lam_done, 2)

            for l in layers(dve):
                chain[0] = 0
                for j in range(KD):
                    dve.wait_ge(u_hi_made, val(u_hi_made, l, j + 1))
                    nc.vector.scalar_tensor_tensor(out=u_lo[:, j, :], in0=h[:, j, :], scalar=cols(g_cols, G_MIX + j, l, KD),
                                                   in1=u_hi[:, j, :].bitcast(F32), op0=ALU.mult, op1=ALU.subtract
                                                   ).then_inc(u_lo_made, 1)
                    add_square(l, j, j == 0)
                stat_col(l, MISC_AT["mix_c"], D_MODEL, EPS)
                stat_diag(l, 0, rs_mix)
                stat_row(l, MISC_AT["mix_b"], rb[:, :])
                for k, use in enumerate(A_USES):
                    b = bank[BANK[use]]
                    dve.wait_ge(proj_done, val(proj_done, l, USE[use] + 1))
                    if use in ("cq0", "cq1", "ckv0", "ckv1"):
                        nc.vector.tensor_tensor(e_t[:, k, :], b[:, :], rb[:, :], ALU.mult).then_inc(freed(use), 1)
                        if use == "cq1":
                            add_square(l, KD, True)
                            add_square(l, KD + 1, False)
                    if use == "kr":
                        link(l, nc.vector.tensor_tensor(ck[0:2 * ROPE, :], tabk[0:2 * ROPE, :], rb[0:2 * ROPE, :], ALU.mult))
                        dve.wait_ge(kr_half, val(kr_half, l, 1))
                        nc.vector.tensor_tensor(krf[0:2 * ROPE, :], b[0:2 * ROPE, :], krf[0:2 * ROPE, :], ALU.add
                                                ).then_inc(freed(use), 1)
                        dve.wait_ge(*read_out(l, use))
                        link(l, nc.vector.tensor_tensor(krf[0:2 * ROPE, :], krf[0:2 * ROPE, :], ck[0:2 * ROPE, :], ALU.mult))
                        link(l, nc.vector.tensor_copy(ck[0:ROPE, :], krf[ROPE:2 * ROPE, :]))
                        nc.vector.tensor_tensor(krf[NOPE:QK, :], krf[0:ROPE, :], ck[0:ROPE, :], ALU.add
                                                ).then_inc(kr_ready, 1)
                    if use[0] == "d":
                        i = A_USES.index(use) - 5
                        if i < DIFF_HEADS:
                            nc.vector.tensor_tensor(tmp_y[:, i % 2, :], b[:, :], rb[:, :], ALU.mult).then_inc(freed(use), 1)
                        else:
                            c = DIFF_D ** -0.5 / SLOPES[i - DIFF_HEADS]
                            nc.vector.scalar_tensor_tensor(out=tmp_y[:, i % 2, :], in0=b[:, :], scalar=c, in1=rb[:, :],
                                                           op0=ALU.mult, op1=ALU.mult).then_inc(freed(use), 1)
                        if use == "dk1":
                            stat_col(l, MISC_AT["q_c"], LORA, EPS)
                            stat_diag(l, 1, rs)
                        if use == "dk2":
                            stat_row(l, MISC_AT["q_b"], rb_c[:, :])
                            add_square(l, KD + 2, True)
                            add_square(l, KD + 3, False)
                            for t in range(KC):
                                nc.vector.scalar_tensor_tensor(out=e_t[:, t, :], in0=e_t[:, t, :],
                                                               scalar=cols(g_cols, G_Q + t, l, KC), in1=rb_c[:, :],
                                                               op0=ALU.mult, op1=ALU.mult).then_inc(c_ready, 1)
                        if use == "dk3":
                            stat_col(l, MISC_AT["kv_c"], LORA, EPS)
                            stat_diag(l, 2, rs)
                        if use == "dq0":
                            stat_row(l, MISC_AT["kv_b"], rb_c[:, :])
                            for t in range(KC, 2 * KC):
                                nc.vector.scalar_tensor_tensor(out=e_t[:, t, :], in0=e_t[:, t, :],
                                                               scalar=cols(g_cols, G_KV + t - KC, l, KC), in1=rb_c[:, :],
                                                               op0=ALU.mult, op1=ALU.mult).then_inc(c_ready, 1)
                        dst, hi = (dk_lo, dk_hi) if i < DIFF_HEADS else (dq_lo, dq_hi)
                        dve.wait_ge(d_hi_made, val(d_hi_made, l, i + 1))
                        nc.vector.tensor_tensor(dst[:, i % DIFF_HEADS, :], tmp_y[:, i % 2, :],
                                                hi[:, i % DIFF_HEADS, :].bitcast(F32), ALU.subtract).then_inc(d_lo_made, 1)
                        if use in ("dq1", "dq2"):
                            for t in (0, 1) if use == "dq1" else (2, 3):
                                dve.wait_ge(c_hi_made, val(c_hi_made, l, t + 1))
                                nc.vector.tensor_tensor(c_lo[:, t, :], e_t[:, t, :], c_hi[:, t, :].bitcast(F32), ALU.subtract
                                                        ).then_inc(c_lo_made, 1)
                    split(l, k + RING)
                for b in range(TT):
                    split(l, BLOCK_AT[("dv", b)] + RING)
                for tt in range(TT):
                    dve.wait_ge(dv_hi_made, val(dv_hi_made, l, tt + 1))
                    nc.vector.scalar_tensor_tensor(out=dv_lo[:, tt, :], in0=DV_BANKS[tt][:, :], scalar=rs_mix[:, tt:tt + 1],
                                                   in1=dv_hi[:, tt, :].bitcast(F32), op0=ALU.mult, op1=ALU.subtract
                                                   ).then_inc(dv_lo_made, 1)
                for n in range(STEPS + 3):
                    if 0 < n <= DSTEPS:
                        coef(l, n - 1)
                    if n < DSTEPS:
                        ttr(l, 2 * n)
                        ttr(l, 2 * n + 1)
                    elif n == DSTEPS:
                        weights(l, n - 1)
                        row_max(l, 0)
                    elif n < STEPS:
                        row_max(l, n - DSTEPS)
                    g, r = divmod(n - 6, TT)
                    if r == 0 and 0 <= g < DIFF_HEADS:
                        stat_col(l, MISC_AT[f"sub{g}_c"], 2 * DIFF_D, SUBLN_EPS)
                    if r == 0 and DIFF_HEADS <= g < DIFF_HEADS + MLA_HEADS - 1:
                        pv_out(l, g)
                    if 0 < n < DSTEPS:
                        weights(l, n - 1)
                    elif DSTEPS < n <= STEPS:
                        normalise(l, n - 1 - DSTEPS)
                    if 2 <= n < STEPS + 2:
                        lo_pt(l, n - 2)
                    if n in (DSTEPS - 1, DSTEPS + 2):
                        for p in (0, 1) if n == DSTEPS - 1 else (2, 3):
                            dve.wait_ge(krb_hi_made, val(krb_hi_made, l, p + 1))
                            nc.vector.tensor_tensor(k_pack[NOPE:QK, p, 1, :], krf[NOPE:QK, :],
                                                    k_pack[NOPE:QK, p, 0, :].bitcast(F32), ALU.subtract
                                                    ).then_inc(krb_lo_made, 1)
                    for use in step_gens(n):
                        gen(l, use)
                        if use[0] == "q":
                            gen_q_low(l, int(use[1:]))
                    if r == 0 and 0 <= g < DIFF_HEADS:
                        stat_diag(l, 3 + g, rs)
                    if r == 2 and 0 <= g < DIFF_HEADS:
                        dve.wait_ge(misc_done, val(misc_done, l, MISC_AT[f"sub{g}_b"] + 1))
                        nc.vector.scalar_tensor_tensor(out=tmp_s[:, 0, :], in0=tmp_s[:, 0, :], scalar=cols(gsl, 0, l),
                                                       in1=MISC_BANK[:, :], op0=ALU.mult, op1=ALU.mult
                                                       ).then_inc(misc_free, 1)
                        o_low(l, g, DIFF_HEADS + g)
                    if r == 1 and g >= DIFF_HEADS and (g - DIFF_HEADS) % 2 == 1 and g < DIFF_HEADS + MLA_HEADS - 1:
                        hd = g - DIFF_HEADS
                        o_low(l, DIFF_HEADS + hd // 2, hd // 2)
                    if n in OUT_SPLITS:
                        split(l, OUT_SPLITS[n])
                pv_out(l, DIFF_HEADS + MLA_HEADS - 1)
                o_low(l, KD - 1, MLA_HEADS // 2 - 1)
                for j in range(KD):
                    use = f"out{j}"
                    dve.wait_ge(proj_done, val(proj_done, l, USE[use] + 1))
                    dve.wait_ge(sq_ready, val(sq_ready, l, j + 1))
                    nc.vector.tensor_tensor(h[:, j, :], h[:, j, :], bank[BANK[use]][:, :], ALU.add).then_inc(freed(use), 1)
                    split(l, BLOCK_AT[(use, 0)] + RING)
                    add_square(l, KD + 2 * KC + j, j == 0)
                for j in range(KD):
                    dve.wait_ge(u_hi_made, val(u_hi_made, l, KD + j + 1))
                    nc.vector.scalar_tensor_tensor(out=u_lo[:, j, :], in0=h[:, j, :], scalar=cols(g_cols, G_MLP + j, l, KD),
                                                   in1=u_hi[:, j, :].bitcast(F32), op0=ALU.mult, op1=ALU.subtract
                                                   ).then_inc(u_lo_made, 1)
                stat_col(l, MISC_AT["mlp_c"], D_MODEL, EPS)
                stat_diag(l, 3 + DIFF_HEADS, rs)
                stat_row(l, MISC_AT["mlp_b"], rb[:, :])
                b = BLOCK_AT[("up0", 0)]
                f = 0
                for kind, c in mlp_order():
                    for i in range(FC):
                        if kind == "up":
                            use = f"up{c}_{i}"
                            dve.wait_ge(proj_done, val(proj_done, l, USE[use] + 1))
                            nc.vector.tensor_tensor(tmp_y[:, 0, :], bank[BANK[use]][:, :], rb[:, :], ALU.mult
                                                    ).then_inc(freed(use), 1)
                            dve.wait_ge(*read_out(l, use))
                            nc.vector.scalar_tensor_tensor(out=tmp_y[:, 1, :], in0=tmp_y[:, 0, :], scalar=0.0,
                                                           in1=tmp_y[:, 0, :], op0=ALU.max, op1=ALU.mult
                                                           ).then_inc(hid_f, 1)
                            f += 1
                        else:
                            for j in (2 * i, 2 * i + 1):
                                use = f"down{c}_{j}"
                                dve.wait_ge(proj_done, val(proj_done, l, USE[use] + 1))
                                nc.vector.tensor_tensor(h[:, j, :], h[:, j, :], bank[BANK[use]][:, :], ALU.add
                                                        ).then_inc(freed(use), 1)
                        if b + RING < NBLK:
                            split(l, b + RING)
                        elif l + 1 < DEPTH:
                            split(l + 1, b + RING - NBLK)
                        b += 1
                        if kind == "up":
                            dve.wait_ge(hid_hi_made, val(hid_hi_made, l, f))
                            nc.vector.tensor_tensor(hid_lo[:, c % 2, i, :], tmp_y[:, 1, :], hid_hi[:, c % 2, i, :].bitcast(F32),
                                                    ALU.subtract).then_inc(hid_lo_made, 1)
                assert chain[0] == CHAIN, chain[0]
            for j in range(KD):
                add_square(DEPTH, j, j == 0)
            stat_col(DEPTH, 0, D_MODEL, EPS)
            stat_diag(DEPTH, 0, rs)
            stat_row(DEPTH, 1, rb[:, :])
            for j in range(KD):
                if j >= 2:
                    dve.wait_ge(yt_done, j - 1)
                nc.vector.scalar_tensor_tensor(out=tmp_y[:, j % 2, :], in0=h[:, j, :],
                                               scalar=g_cols[:, G_FINAL + j:G_FINAL + j + 1],
                                               in1=rb[:, :], op0=ALU.mult, op1=ALU.mult).then_inc(y_ready, 1)
                if j:
                    dve.wait_ge(yt_done, j)
                    nc.vector.tensor_copy(yout[:, :, (j - 1) * P:j * P], bank[(j - 1) % 4].rearrange("p (t c) -> p t c", t=TT)
                                          ).then_inc(y_copied, 1)
            dve.wait_ge(yt_done, KD)
            nc.vector.tensor_copy(yout[:, :, (KD - 1) * P:], bank[(KD - 1) % 4].rearrange("p (t c) -> p t c", t=TT)
                                  ).then_inc(y_copied, 1)

        @block.tensor
        def _(pe):
            def three(acc, terms, first, last):
                for t, ((a_hi, a_lo), (b_hi, b_lo)) in enumerate(terms):
                    for m, (a, b) in enumerate(((a_hi, b_hi), (a_hi, b_lo), (a_lo, b_hi))):
                        mm = nc.tensor.matmul(acc, a, b, start=first and t == 0 and m == 0,
                                              stop=last and t == len(terms) - 1 and m == 2)
                return mm

            def wtile(s, k, w=P):
                return w_hi[:, s, k * w:(k + 1) * w], w_lo[:, s, k * w:(k + 1) * w]

            def u(k):
                return u_hi[:, k, :], u_lo[:, k, :]

            def stat_c(l, m, src=None):
                pe.wait_ge(misc_free, val(misc_free, l, m))
                for tt in range(TT):
                    mm = nc.tensor.matmul(MISC_BANK[:, tt:tt + 1], (ss[:, tt * P:(tt + 1) * P] if src is None
                                                                   else src[:, tt * P:(tt + 1) * P]),
                                          ones[:, 0:1], start=True, stop=True)
                mm.then_inc(misc_done, 1)

            def stat_b(l, m, k):
                pe.wait_ge(diag_ready, val(diag_ready, l, k + 1))
                pe.wait_ge(misc_free, val(misc_free, l, m))
                nc.tensor.matmul(MISC_BANK[:, :], ones[:, :], diag.rearrange("p t c -> p (t c)"), start=True, stop=True
                                 ).then_inc(misc_done, 1)

            def scores(l, n):
                if n < DSTEPS:
                    hd, qt = divmod(n, TT)
                    if qt == 0:
                        pe.wait_ge(d_lo_made, val(d_lo_made, l, DIFF_HEADS + hd + 1))
                    for m in range(2):
                        e = 2 * n + m
                        pe.wait_ge(sc_free, val(sc_free, l, e - 2))
                        rows = slice(m * DIFF_D, (m + 1) * DIFF_D)
                        three(SC_BANKS[e % 3][:, :],
                              [((dq_hi[rows, hd, qt * P:(qt + 1) * P], dq_lo[rows, hd, qt * P:(qt + 1) * P]),
                                (dk_hi[rows, hd, :], dk_lo[rows, hd, :]))], True, True).then_inc(sc_done, 1)
                else:
                    hd, qt = divmod(n - DSTEPS, TT)
                    e = 2 * DSTEPS + n - DSTEPS
                    if qt == 0:
                        pe.wait_ge(q_lo_made, val(q_lo_made, l, hd + 1))
                        pe.wait_ge(krb_lo_made, val(krb_lo_made, l, 2 if hd < 2 else 4))
                        pe.wait_ge(*read_out(l, f"kp{hd // 2}"))
                    pe.wait_ge(sc_free, val(sc_free, l, e - 2))
                    b = hd % 2
                    three(SC_BANKS[e % 3][:, :],
                          [((q_hi[0:QK, b, qt * P:(qt + 1) * P], q_lo[0:QK, b, qt * P:(qt + 1) * P]),
                            (k_pack[0:QK, hd % 4, 0, :], k_pack[0:QK, hd % 4, 1, :]))], True, True).then_inc(sc_done, 1)

            def turn(l, n):
                t = 2 * (n % 2) if n < DSTEPS else (n - DSTEPS) % 4
                pe.wait_ge(w_ready, val(w_ready, l, n + 1))
                pe.wait_ge(pt_lo_made, val(pt_lo_made, l, n - 1))
                for kt in range(TT):
                    mm = nc.tensor.transpose(TR_BANKS[n % 2][:, kt * P:(kt + 1) * P], e_t[:, t, kt * P:(kt + 1) * P],
                                             ident[:, :])
                mm.then_inc(tr_done, 1)

            def values(l, g):
                m = MISC_AT[f"pv{g}"]
                pe.wait_ge(pt_lo_made, val(pt_lo_made, l, TT * (g + 1)))
                pe.wait_ge(misc_free, val(misc_free, l, m))
                if g < DIFF_HEADS:
                    c = slice(g * 2 * DIFF_D, (g + 1) * 2 * DIFF_D)
                    three(MISC_BANK[:, :], [((dv_hi[:, kt, c], dv_lo[:, kt, c]), (pt_hi[:, kt, :], pt_lo[:, kt, :]))
                                            for kt in range(TT)], True, True).then_inc(misc_done, 1)
                    return
                hd = g - DIFF_HEADS
                if hd == 0:
                    for tt in range(TT):
                        pe.wait_ge(*read_out(l, f"v{tt}"))
                for kt in range(TT):
                    for pt in (pt_hi, pt_lo):
                        mm = nc.tensor.matmul(MISC_BANK[:, :], v_pack[:, kt, hd, :, :].rearrange("p a c -> p (a c)"),
                                              pt[:, kt, :], start=(kt == 0 and pt is pt_hi), stop=(kt == TT - 1 and pt is pt_lo))
                mm.then_inc(misc_done, 1)

            def gen(l, use):
                pe.wait_ge(*taken(l, use))
                acc = bank[BANK[use]][:, :]
                slot = {("uq", k): SLOT[BLOCK_AT[("uq", k)]] for k in range(KC)}
                slot.update({("ukv", k): SLOT[BLOCK_AT[("ukv", k)]] for k in range(KC)})
                i = int(use.lstrip("vqkp"))
                terms = []
                for k in range(KC):
                    pe.wait_ge(w_hi_made, val(w_hi_made, l, BLOCK_AT[("uq" if use[0] == "q" else "ukv", k)] + 1))
                    pe.wait_ge(w_lo_made, val(w_lo_made, l, BLOCK_AT[("uq" if use[0] == "q" else "ukv", k)] + 1))
                    if use[0] == "q":
                        terms.append((wtile(slot[("uq", k)], i), (c_hi[:, k, :], c_lo[:, k, :])))
                        continue
                    wv = [t[:, slot[("ukv", k)], :] for t in (w_hi, w_lo)]
                    if use[0] == "k":
                        terms.append((tuple(w[:, i * P:(i + 1) * P] for w in wv), (c_hi[:, KC + k, :], c_lo[:, KC + k, :])))
                    else:
                        terms.append((tuple(c[:, KC + k, i * P:(i + 1) * P] for c in (c_hi, c_lo)),
                                      tuple(w[:, MLA_HEADS * NOPE:] for w in wv)))
                three(acc, terms, True, True).then_inc(proj_done, 1)

            pe.wait_ge(consts_made, 4)
            pe.wait_ge(g_in, 160)
            nc.tensor.transpose(bank[6][:, 0:G_ROWS], g_rows[0:G_ROWS, :], ident[0:G_ROWS, 0:G_ROWS]).then_inc(gt_done, 1)
            for j in range(KD):
                pe.wait_ge(x_in, 32)
                if j >= 4:
                    pe.wait_ge(bank_free[j % 4], val(bank_free[j % 4], -1, -1 + BANK_USES[j % 4]))
                for tt in range(TT):
                    mm = nc.tensor.transpose(bank[j % 4][:, tt * P:(tt + 1) * P], xin[:, tt, j * P:(j + 1) * P], ident[:, :])
                mm.then_inc(xt_done, 1)
            pe.wait_ge(lam_m, 1)
            nc.tensor.matmul(bank[7][:, 0:DEPTH], ones[0:4, :], lam_s[:, 2:2 + DEPTH], start=True, stop=True
                             ).then_inc(lam_m, 1)

            for l in layers(pe):
                for k, use in enumerate(A_USES):
                    pe.wait_ge(w_hi_made, val(w_hi_made, l, BLOCK_AT[(use, 0)] + 1))
                    pe.wait_ge(w_lo_made, val(w_lo_made, l, BLOCK_AT[(use, 0)] + 1))
                    if k < 3:
                        pe.wait_ge(sc_free, val(sc_free, l, 0))
                        for b in range(4):
                            pe.wait_ge(bank_free[b], val(bank_free[b], l, 0))
                    pe.wait_ge(*taken(l, use))
                    acc = bank[BANK[use]][:, :]
                    s = SLOT[k]
                    if use == "kr":
                        first = True
                        for t in range(KD):
                            for m in range(2):
                                mm = nc.tensor.matmul(acc, w_hi[:, s, t * P:(t + 1) * P], u(t)[m], start=first,
                                                      stop=(t == KD - 1 and m == 1))
                                first = False
                    else:
                        for t in range(KD):
                            if k == 0:
                                pe.wait_ge(u_lo_made, val(u_lo_made, l, t + 1))
                            mm = three(acc, [(wtile(s, t), u(t))], t == 0, t == KD - 1)
                    mm.then_inc(proj_done, 1)
                    if use == "cq0":
                        pe.wait_ge(ss_acc, val(ss_acc, l, KD))
                        stat_c(l, MISC_AT["mix_c"])
                    if use == "cq1":
                        stat_b(l, MISC_AT["mix_b"], 0)
                    if use == "dk0":
                        pe.wait_ge(ss_acc, val(ss_acc, l, KD + 2))
                        stat_c(l, MISC_AT["q_c"])
                    if use == "dk1":
                        stat_b(l, MISC_AT["q_b"], 1)
                    if use == "dk2":
                        pe.wait_ge(ss_acc, val(ss_acc, l, KD + 4))
                        stat_c(l, MISC_AT["kv_c"])
                    if use == "dk3":
                        stat_b(l, MISC_AT["kv_b"], 2)
                pe.wait_ge(pt_lo_made, val(pt_lo_made, l, 0))
                for b in range(TT):
                    pe.wait_ge(w_hi_made, val(w_hi_made, l, BLOCK_AT[("dv", b)] + 1))
                    pe.wait_ge(w_lo_made, val(w_lo_made, l, BLOCK_AT[("dv", b)] + 1))
                    s = SLOT[BLOCK_AT[("dv", b)]]
                    for tt in range(TT):
                        for k in range(2):
                            kk = 2 * b + k
                            mm = three(DV_BANKS[tt][:, :], [(tuple(t[:, kk, tt * P:(tt + 1) * P] for t in (u_hi, u_lo)),
                                                             wtile(s, k, SEQ))], kk == 0, kk == KD - 1)
                    mm.then_inc(dv_done, 1)
                for use in A_USES[-3:]:
                    pe.wait_ge(*read_out(l, use))
                pe.wait_ge(dv_lo_made, val(dv_lo_made, l, TT))
                scores(l, 0)
                scores(l, 1)
                for n in range(STEPS + 1):
                    if n + 2 < DSTEPS or DSTEPS <= n < STEPS - 2:
                        scores(l, n + 2)
                    g, r = divmod(n - TT, TT)
                    if r == 0 and g >= 0:
                        values(l, g)
                    if n in (DSTEPS - 2, DSTEPS - 1):
                        if n == DSTEPS - 2:
                            pe.wait_ge(c_lo_made, val(c_lo_made, l, 2 * KC))
                        for use in gen_uses(n):
                            gen(l, use)
                    if n < STEPS:
                        turn(l, n)
                    if n == DSTEPS - 1:
                        scores(l, DSTEPS)
                        scores(l, DSTEPS + 1)
                    if n >= DSTEPS:
                        for use in gen_uses(n):
                            gen(l, use)
                    if r == 0 and 0 <= g < DIFF_HEADS:
                        stat_c(l, MISC_AT[f"sub{g}_c"], tmp_s[:, 1, :])
                    if r == 2 and 0 <= g < DIFF_HEADS:
                        stat_b(l, MISC_AT[f"sub{g}_b"], 3 + g)
                pe.wait_ge(sc_free, val(sc_free, l, 2 * DSTEPS + MSTEPS))
                for j, use in enumerate(OUT_USES):
                    pe.wait_ge(w_hi_made, val(w_hi_made, l, BLOCK_AT[(use, 0)] + 1))
                    pe.wait_ge(w_lo_made, val(w_lo_made, l, BLOCK_AT[(use, 0)] + 1))
                    pe.wait_ge(*taken(l, use))
                    s = SLOT[BLOCK_AT[(use, 0)]]
                    order = list(range(KD // 2, KD)) + list(range(KD // 2))
                    for t, k in enumerate(order):
                        if j == 0:
                            pe.wait_ge(o_lo_made, val(o_lo_made, l, t + 1))
                        mm = three(bank[BANK[use]][:, :], [(wtile(s, k), u(k))], t == 0, t == KD - 1)
                    mm.then_inc(proj_done, 1)
                f = 0
                for kind, c in mlp_order():
                    for i in range(FC):
                        key = (f"{kind}{c}", i)
                        s = SLOT[BLOCK_AT[key]]
                        pe.wait_ge(w_hi_made, val(w_hi_made, l, BLOCK_AT[key] + 1))
                        pe.wait_ge(w_lo_made, val(w_lo_made, l, BLOCK_AT[key] + 1))
                        if kind == "up":
                            use = f"up{c}_{i}"
                            pe.wait_ge(*taken(l, use))
                            for t in range(KD):
                                if c == 0 and i == 0:
                                    pe.wait_ge(u_lo_made, val(u_lo_made, l, KD + t + 1))
                                mm = three(bank[BANK[use]][:, :], [(wtile(s, t), u(t))], t == 0, t == KD - 1)
                            mm.then_inc(proj_done, 1)
                            if c == 0 and i == 0:
                                pe.wait_ge(ss_acc, val(ss_acc, l, 2 * KD + 2 * KC))
                                stat_c(l, MISC_AT["mlp_c"])
                            if c == 0 and i == 1:
                                stat_b(l, MISC_AT["mlp_b"], 3 + DIFF_HEADS)
                            continue
                        for j in range(2):
                            use = f"down{c}_{2 * i + j}"
                            pe.wait_ge(*taken(l, use))
                            for t in range(FC):
                                if i == 0 and j == 0:
                                    pe.wait_ge(hid_lo_made, val(hid_lo_made, l, c * FC + t + 1))
                                w = tuple(x[:, s, t * 256 + j * P:t * 256 + (j + 1) * P] for x in (w_hi, w_lo))
                                mm = three(bank[BANK[use]][:, :], [(w, (hid_hi[:, c % 2, t, :], hid_lo[:, c % 2, t, :]))],
                                           t == 0, t == FC - 1)
                            mm.then_inc(proj_done, 1)
            pe.wait_ge(ss_acc, val(ss_acc, DEPTH, KD))
            stat_c(DEPTH, 0)
            stat_b(DEPTH, 1, 0)
            for j in range(KD):
                pe.wait_ge(y_ready, j + 1)
                if j < 4:
                    pe.wait_ge(bank_free[j], val(bank_free[j], DEPTH, 0))
                else:
                    pe.wait_ge(y_copied, j - 3)
                for tt in range(TT):
                    mm = nc.tensor.transpose(bank[j % 4][:, tt * P:(tt + 1) * P], tmp_y[:, j % 2, tt * P:(tt + 1) * P],
                                             ident[:, :])
                mm.then_inc(yt_done, 1)


def step_gens(n):
    if n == DSTEPS - 1:
        return gen_uses(n - 1)
    if n == DSTEPS:
        return gen_uses(n - 1)
    return gen_uses(n - 2) if n >= DSTEPS + 2 else []


LAST_GEN = max(n for n in range(STEPS) if gen_uses(n))
OUT_SPLITS = {LAST_GEN + 3 + 2 * i: BLOCK_AT[(f"out{i}", 0)] for i in range(RING)}


_INS = ["x", "w_in", "g_mix", "g_q", "g_kv", "w_uq", "w_ukv", "lam_q1", "lam_k1", "lam_q2", "lam_k2",
        "g_sub", "w_out", "g_mlp", "w_up", "w_down", "g_final"]


def shape_constants(np):
    f = np.float32
    pos = np.arange(SEQ, dtype=f)
    inv = (f(1.0) / (f(ROPE_THETA) ** (np.arange(0, ROPE, 2, dtype=f) / f(ROPE)))).astype(f)
    ang = (pos[:, None] * inv[None, :]).astype(f)
    cos, sin = np.cos(ang).T, np.sin(ang).T
    c = np.zeros((P, C_W), f)
    scale = f(QK ** -0.5)
    c[0:NOPE, C_TABQ:C_TABQ + SEQ] = scale
    c[NOPE:QK, C_TABQ:C_TABQ + SEQ] = np.concatenate([cos, cos]) * scale
    c[QK:P, C_TABQ:C_TABQ + SEQ] = np.concatenate([-sin, sin]) * scale
    c[0:ROPE, C_TABK:C_TABK + SEQ] = np.concatenate([cos, cos])
    c[ROPE:2 * ROPE, C_TABK:C_TABK + SEQ] = np.concatenate([-sin, sin])
    c[:, C_NEGD:C_NEGD + NEGD] = -np.abs(np.arange(P)[:, None] + (TT - 1) * P - np.arange(NEGD)[None, :])
    for l in range(DEPTH):
        c[l, C_SIGN + l], c[DEPTH + l, C_SIGN + l] = 1.0, -1.0
        lam_init = 0.8 - 0.6 * math.exp(-0.3 * l)
        c[:, C_INIT + l] = lam_init
        c[:, C_GSC + l] = 1.0 - lam_init
    return c


def kernel(**inputs):
    import numpy as np
    import concourse.bacc as bacc
    from concourse.bass_utils import run_bass_kernel_spmd

    nc = bacc.Bacc("TRN2", target_bir_lowering=False, num_devices=1)
    arrays, args = {}, []
    for name in _INS:
        a = np.ascontiguousarray(inputs[name])
        arrays[f"in_{name}"] = a
        args.append(nc.dram_tensor(f"in_{name}", a.shape, mybir.dt.from_np(a.dtype), kind="ExternalInput").ap())
    c = shape_constants(np)
    arrays["in_cst"] = c
    args.append(nc.dram_tensor("in_cst", c.shape, F32, kind="ExternalInput").ap())
    args.append(nc.dram_tensor("out_0", (1, SEQ, D_MODEL), F32, kind="ExternalOutput").ap())
    trunk(nc, *args)
    r = run_bass_kernel_spmd(nc, [arrays], core_ids=[0])
    return r.results[0]["out_0"]
```

```python
import math
from contextlib import ExitStack

import concourse.bass as bass
from concourse import mybir

F32 = mybir.dt.float32
F32R = mybir.dt.float32r
ALU = mybir.AluOpType
ACT = mybir.ActivationFunctionType
AX_X = mybir.AxisListType.X

P = 128
SEQ, D_MODEL, DEPTH = 512, 1024, 2
KD = D_MODEL // P
TT = SEQ // P
MLA_HEADS, NOPE, ROPE, MLA_V = 8, 64, 32, 64
LORA = 256
KC = LORA // P
DIFF_HEADS, DIFF_D = 4, 64
D_FF = 4 * D_MODEL
QK = NOPE + ROPE
DIFF_W = DIFF_HEADS * 2 * DIFF_D
OFF_CQ, OFF_CKV, OFF_KR = 0, LORA, 2 * LORA
OFF_DQ = OFF_KR + ROPE
OFF_DK = OFF_DQ + DIFF_W
OFF_DV = OFF_DK + DIFF_W
P_IN = OFF_DV + DIFF_W
EPS, SUBLN_EPS = 1e-6, 1e-5
ROPE_THETA = 10000.0
FC = 4
CHUNKS = D_FF // (FC * P)
BLK = 1024
NEGD = SEQ + (TT - 1) * P

C_TABQ, C_TABK, C_NEGD = 0, SEQ, 2 * SEQ
C_SIGN = C_NEGD + NEGD
C_INIT = C_SIGN + DEPTH
C_GSC = C_INIT + DEPTH
C_W = C_GSC + DEPTH

G_MIX, G_MLP = 0, DEPTH * KD
G_FINAL = 2 * DEPTH * KD
G_Q = G_FINAL + KD
G_KV = G_Q + DEPTH * KC
G_SUB = G_KV + DEPTH * KC
G_ROWS = G_SUB + DEPTH

SLOPES = [2.0 ** (-8.0 * (h + 1) / DIFF_HEADS) for h in range(DIFF_HEADS)]
DSTEPS = DIFF_HEADS * TT
MSTEPS = MLA_HEADS * TT
STEPS = DSTEPS + MSTEPS

LATENT_USES = ["cq0", "cq1", "ckv0", "ckv1", "kr"]
HEAD_USES = [f"{d}{g}" for g in range(DIFF_HEADS) for d in ("dk", "dq")]
FIRST_USES = HEAD_USES[:2]
SECOND_USES = HEAD_USES[2:4]


def fillers():
    fill = {n: [] for n in range(STEPS)}
    for g in range(2, DIFF_HEADS):
        n = TT * (g - 2)
        for use in (f"dk{g}", f"dq{g}"):
            fill[n].append((use, range(0, KD // 2)))
            fill[n + 1].append((use, range(KD // 2, KD)))
            n += 2
    for use, n in (("q0", 9), ("kp0", 11), ("v0", 12), ("v1", 13), ("q1", 15), ("v2", 16), ("v3", 18)):
        fill[n].append((use, range(KC)))
    for hd in range(MLA_HEADS - 2):
        n = DSTEPS + 1 + TT * hd
        if hd % 2 == 0:
            fill[n + 2].append((f"kp{hd // 2 + 1}", range(KC)))
        fill[n].append((f"q{hd + 2}", range(KC)))
    for j, (a, b) in enumerate(OUTD_STEPS):
        fill[a].append((f"outd{j}", range(0, 2)))
        fill[b].append((f"outd{j}", range(2, TT)))
    return fill


OUTD_STEPS = [(23, 24), (27, 28), (31, 32), (35, 36), (39, 40), (41, 42), (43, 44), (45, 46)]
FILL = fillers()


def ended(n):
    if n == -1:
        return SECOND_USES
    if n not in FILL:
        return []
    return [u for u, part in FILL[n] if part[-1] == {"o": TT, "d": KD}.get(u[0], KC) - 1]


FILL_USES = [u for n in range(STEPS) for u in ended(n)]
LAST_Q = f"q{MLA_HEADS - 1}"
HALVES = list(range(KD // 2, KD)) + list(range(KD // 2))
OUTM_USES = [f"outm{j}" for j in HALVES]


def mlp_order():
    order = [("up", 0)]
    for c in range(CHUNKS):
        if c + 1 < CHUNKS:
            order.append(("up", c + 1))
        order.append(("down", c))
    return order


MLP_USES = [f"{kind}{c}_{i}" for kind, c in mlp_order() for i in range(FC if kind == "up" else KD)]
EARLY_USES = LATENT_USES + FIRST_USES + SECOND_USES + FILL_USES
USES = EARLY_USES + OUTM_USES + MLP_USES
USE = {u: k for k, u in enumerate(USES)}
BANK = {}
for names, banks in ((LATENT_USES, (0, 1, 2, 3)), (FIRST_USES + SECOND_USES + FILL_USES, (1, 0)), (OUTM_USES, (1, 0, 2, 3)),
                     (MLP_USES, (0, 1, 2, 3))):
    for k, u in enumerate(names):
        BANK[u] = banks[k % len(banks)]
NTH = {}
BANK_USES = [0] * 4
for u in USES:
    NTH[u] = BANK_USES[BANK[u]]
    BANK_USES[BANK[u]] += 1

MISC = ["mix_c", "mix_b", "q_c", "q_b", "kv_c", "kv_b"]
for g in range(DIFF_HEADS):
    MISC += [f"pv{g}", f"sub{g}_c", f"sub{g}_b"]
MISC += [f"pv{DIFF_HEADS + h}" for h in range(MLA_HEADS)] + ["mlp_c", "mlp_b"]
MISC_AT = {m: k for k, m in enumerate(MISC)}

BLOCKS = [(u, 0) for u in LATENT_USES] + [("dv", b) for b in range(TT)] + [(u, 0) for u in HEAD_USES]
BLOCKS += [("uq", 0), ("uq", 1), ("ukv", 0), ("ukv", 1)]
BLOCKS += [("outd", i) for i in range(TT)] + [("outm", i) for i in (2, 3, 0, 1)]
for kind, c in mlp_order():
    BLOCKS += [(f"{kind}{c}", i) for i in range(FC)]
BLOCK_AT = {b: k for k, b in enumerate(BLOCKS)}
NBLK = len(BLOCKS)
STAGES = 2
RING = 4
SLOTS = RING + 1

OUTD_AT, OUTM_AT = BLOCK_AT[("outd", 0)], BLOCK_AT[("outm", 2)]
SLOT = [b % RING if b < OUTD_AT else
        RING if b < OUTM_AT - 1 else
        RING - 1 if b < OUTM_AT else
        (b - OUTM_AT) % RING for b in range(NBLK)]
STAGE = [b % STAGES for b in range(NBLK)]
assert (NBLK - OUTM_AT) % RING == 0
assert SLOT[BLOCK_AT[("ukv", 0)]] == RING - 1


def previous(b, slots=SLOT):
    before = [a for a in range(b) if slots[a] == slots[b]]
    if before:
        return before[-1]
    return max(a for a in range(NBLK) if slots[a] == slots[b]) - NBLK


CHAIN = 3 + DSTEPS

def trunk(nc, x, w_in, g_mix, g_q, g_kv, w_uq, w_ukv, lam_q1, lam_k1, lam_q2, lam_k2,
          g_sub, w_out, g_mlp, w_up, w_down, g_final, cst, out):
    at_byte = [16512]

    def place(name, shape, dt, at=None):
        size = 4 * int(math.prod(shape[1:]))
        if at is None:
            at = at_byte[0]
            at_byte[0] += -(-size // 32) * 32
        return nc.alloc_sbuf_tensor_at(name, shape, dt, offset=at)

    h = place("h", [P, KD, SEQ], F32)
    u_hi = place("u_hi", [P, KD, SEQ], F32R)
    u_lo = place("u_lo", [P, KD, SEQ], F32R)
    region = at_byte[0]
    dq_hi = place("dq_hi", [P, DIFF_HEADS, SEQ], F32R)
    dq_lo = place("dq_lo", [P, DIFF_HEADS, SEQ], F32R)
    dk_last = place("dk_last", [P, 2, SEQ], F32R)
    dk_hi = place("dk_hi", [P, DIFF_HEADS - 1, SEQ], F32R)
    dk_lo = place("dk_lo", [P, DIFF_HEADS - 1, SEQ], F32R)
    dv_hi = place("dv_hi", [P, TT, SEQ], F32R)
    dv_lo = place("dv_lo", [P, TT, SEQ], F32R)
    kb = 1024
    v_pack = place("v_pack", [P, TT, MLA_HEADS, 2, MLA_V], F32R, region - 24 * kb)
    q_pack = place("q_pack", [P, 2, 2, SEQ], F32R, region + 16 * kb)
    k_pack = place("k_pack", [P, 4, 2, SEQ], F32R, region + 24 * kb)
    hid_hi = place("hid_hi", [P, 2, FC, SEQ], F32R, region + 16 * kb)
    hid_lo = place("hid_lo", [P, 2, FC, SEQ], F32R, region + 32 * kb)
    xin = place("xin", [P, TT, D_MODEL], F32, region)
    gh = place("gh", [P, KD, SEQ], F32, region - 32 * kb)
    yout = place("yout", [P, TT, D_MODEL], F32, region + 32 * kb)
    c_hi = place("c_hi", [P, 2 * KC, SEQ], F32R)
    c_lo = place("c_lo", [P, 2 * KC, SEQ], F32R)
    stage = place("stage", [P, STAGES, BLK], F32)
    w_at = at_byte[0]
    w_hi = place("w_hi", [P, SLOTS, BLK], F32R)
    w_lo = place("w_lo", [P, SLOTS, BLK], F32R)
    pt_hi = place("pt_hi", [P, TT, SEQ], F32R)
    pt_lo = place("pt_lo", [P, TT, SEQ], F32R)
    scratch = at_byte[0] - 16 * kb
    ss = place("ss", [P, SEQ], F32, scratch)
    rb_c = place("rb_c", [P, SEQ], F32, scratch + 2 * kb)
    ck = place("ck", [P, SEQ], F32, scratch + 4 * kb)
    e_t = place("e_t", [P, 4, SEQ], F32)
    e_x = place("e_x", [P, 2, SEQ], F32, w_at + RING * 4 * BLK)
    tmp_s = place("tmp_s", [P, 2, SEQ], F32)
    tmp_y = place("tmp_y", [P, 2, SEQ], F32)
    rb = place("rb", [P, SEQ], F32)
    krf = place("krf", [P, SEQ], F32)
    consts = place("consts", [P, C_W], F32)
    ident = place("ident", [P, P], F32)
    ones = place("ones", [P, P], F32)
    diag = place("diag", [P, TT, P], F32)
    mhalf = place("mhalf", [P, TT], F32)
    rc = place("rc", [P, TT], F32)
    rs = place("rs", [P, TT], F32)
    rs_mix = place("rs_mix", [P, TT], F32)
    g_rows = place("g_rows", [P, P], F32, region + 16 * kb)
    g_cols = place("g_cols", [P, G_ROWS], F32)
    gsl = place("gsl", [P, DEPTH], F32)
    lam_r = place("lam_r", [4, 2, DIFF_D], F32, region + 17 * kb)
    lam_s = place("lam_s", [4, 4], F32)
    lam_b = place("lam_b", [P, DEPTH], F32)
    nmx = place("nmx", [P, 6], F32)
    rsum = place("rsum", [P, 6], F32)
    coefs = place("coefs", [P, 6], F32)

    tabq = consts[:, C_TABQ:C_TABQ + SEQ]
    tabk = consts[:, C_TABK:C_TABK + SEQ]
    sign = consts[0:4, C_SIGN:C_SIGN + DEPTH]

    with ExitStack() as ctx:
        bank = [ctx.enter_context(nc.psum_tensor(f"bank{b}", [P, SEQ], F32)) for b in range(8)]
        MISC_BANK, SC_BANKS, TR_BANKS, DV_BANKS = bank[5], bank[2:5], bank[6:8], [bank[2], bank[3], bank[6], bank[7]]
        Y_BANKS = ([bank[b] for b in (4, 6, 7, 0)], [bank[b] for b in (1, 2, 3, 5)])
        per_layer, counters = {}, []

        def counter(name, per):
            sem = ctx.enter_context(nc.semaphore(name))
            per_layer[id(sem)] = per
            counters.append(sem)
            return sem

        def once(name):
            return ctx.enter_context(nc.semaphore(name))

        stage_full = [once(f"stage_full{s}") for s in range(STAGES)]
        w_hi_made, w_lo_made = counter("w_hi_made", NBLK), counter("w_lo_made", NBLK)
        proj_done = counter("proj_done", len(USES))
        bank_free = [counter(f"bank{b}_free", BANK_USES[b]) for b in range(4)]
        misc_done, misc_free = counter("misc_done", len(MISC)), counter("misc_free", len(MISC))
        u_hi_made, u_lo_made = counter("u_hi_made", 2 * KD), counter("u_lo_made", 2 * KD)
        sq_ready, ss_acc = counter("sq_ready", 2 * KD + 2 * KC), counter("ss_acc", 2 * KD + 2 * KC)
        pow_done, diag_ready = counter("pow_done", 4 + DIFF_HEADS), counter("diag_ready", 4 + DIFF_HEADS)
        c_ready, c_hi_made, c_lo_made = (counter(n, 2 * KC) for n in ("c_ready", "c_hi_made", "c_lo_made"))
        kr_half, kr_ready = counter("kr_half", 1), counter("kr_ready", 1)
        krb_hi_made, krb_lo_made, krb_copied = counter("krb_hi_made", 4), counter("krb_lo_made", 1), counter("krb_copied", 3)
        d_hi_made, d_lo_made = counter("d_hi_made", 2 * DIFF_HEADS), counter("d_lo_made", 2 * DIFF_HEADS)
        dv_done, dv_hi_made, dv_lo_made = (counter(n, TT) for n in ("dv_done", "dv_hi_made", "dv_lo_made"))
        v_hi_made, k_hi_made = counter("v_hi_made", TT), counter("k_hi_made", MLA_HEADS)
        qf_ready, q_hi_made, q_lo_made = (counter(n, MLA_HEADS) for n in ("qf_ready", "q_hi_made", "q_lo_made"))
        sc_done, sc_free = (counter(n, 2 * DSTEPS + MSTEPS) for n in ("sc_done", "sc_free"))
        mx_ready, e_ready = counter("mx_ready", MSTEPS), counter("e_ready", 2 * DSTEPS)
        coef_ready, t1_ready, w_ready = counter("coef_ready", STEPS), counter("t1_ready", DSTEPS), counter("w_ready", DSTEPS)
        p_ready = counter("p_ready", MSTEPS)
        tr_done, pt_hi_made, pt_lo_made = (counter(n, STEPS) for n in ("tr_done", "pt_hi_made", "pt_lo_made"))
        o_half = counter("o_half", MLA_HEADS)
        o_hi_made, o_lo_made = counter("o_hi_made", KD), counter("o_lo_made", KD)
        hid_f, hid_hi_made, hid_lo_made = (counter(n, CHUNKS * FC) for n in ("hid_f", "hid_hi_made", "hid_lo_made"))
        chain_done = counter("chain_done", CHAIN)
        x_in = [once(f"x_in{j}") for j in range(KD // 2)]
        c_in, g_in, lam_in, consts_made = once("c_in"), once("g_in"), once("lam_in"), once("consts_made")
        xt_done, gt_done, gt_copied = once("xt_done"), once("gt_done"), once("gt_copied")
        lam_e, lam_m, lam_done = once("lam_e"), once("lam_m"), once("lam_done")
        gh_made, yt_done, y_left, y_right, y_out = (once(n) for n in ("gh_made", "yt_done", "y_left", "y_right", "y_out"))

        def val(sem, l, k):
            return (l + 1) * per_layer[id(sem)] + k

        def freed(use):
            return bank_free[BANK[use]]

        def read_out(l, use):
            return freed(use), val(freed(use), l, NTH[use] + 1)

        def taken(l, use):
            return freed(use), val(freed(use), l, NTH[use])

        def stream_ready(l, j):
            return read_out(l - 1, f"down{CHUNKS - 1}_{j}")

        def block_used(l, b):
            if b < 0:
                l, b = l - 1, b + NBLK
            name, i = BLOCKS[b]
            if name == "dv":
                return dv_done, val(dv_done, l, i + 1)
            use = name
            if name in ("uq", "ukv"):
                use = LAST_Q
            elif name in ("outd", "outm"):
                use = f"{name}{2 * i + 1}"
            elif name.startswith("up"):
                use = f"{name}_{i}"
            elif name.startswith("down"):
                use = f"{name}_{2 * i + 1}"
            return proj_done, val(proj_done, l, USE[use] + 1)

        def staged(l, b):
            s = STAGE[b]
            return stage_full[s], (l * STAGE.count(s) + STAGE[:b].count(s) + 1) * 16

        def o_tile(n):
            if n < DIFF_HEADS:
                return dq_hi[:, n, :], dq_lo[:, n, :]
            return u_hi[:, n - DIFF_HEADS, :], u_low(n - DIFF_HEADS)

        def d_keys(g):
            if g == DIFF_HEADS - 1:
                return dk_last[:, 0, :], dk_last[:, 1, :]
            return dk_hi[:, g, :], dk_lo[:, g, :]

        def q_tile(hd):
            return q_pack[0:QK, (hd + 1) % 2, 0, :], q_pack[0:QK, (hd + 1) % 2, 1, :]

        def p_slot(i):
            return (i + 2) % 4

        def e_slot(t):
            return e_t[:, t, :] if t < 4 else e_x[:, t - 4, :]

        def u_low(k):
            return u_lo[:, (k + KD // 2) % KD, :]

        def layers(eng):
            return range(DEPTH)

        def cols(tile, base, l, per=1):
            return tile[:, bass.ds(l * per + base, 1)]

        def block_parts(b):
            name, _ = BLOCKS[b]
            if name == "kr":
                hi = lambda t, s: t[:, s, :].rearrange("p (k c) -> p k c", k=KD)
                st = lambda s: stage[:, s, 0:KD * ROPE].rearrange("p (k c) -> p k c", k=KD)
                half = ROPE // 2
                return hi, st, [(0, 0, ROPE), (ROPE, half, half), (ROPE + half, 0, half)]
            if name == "uq":
                hi = lambda t, s: t[:, s, :].rearrange("p (h c) -> p h c", h=MLA_HEADS)
                st = lambda s: stage[:, s, 0:MLA_HEADS * QK].rearrange("p (h c) -> p h c", h=MLA_HEADS)
                half = ROPE // 2
                return hi, st, [(0, 0, QK), (QK, NOPE + half, half), (QK + half, NOPE, half)]
            if name == "ukv":
                hi = lambda t, s: t[:, s, :].rearrange("p (a h c) -> p h a c", a=2, h=MLA_HEADS)
                st = lambda s: stage[:, s, :].rearrange("p (h a c) -> p h a c", a=2, h=MLA_HEADS)
                return hi, st, [(0, 0, 2)]
            hi = lambda t, s: t[:, s:s + 1, :]
            st = lambda s: stage[:, s:s + 1, :]
            return hi, st, [(0, 0, BLK)]

        block = ctx.enter_context(nc.Block())

        @block.sync
        def _(sp):
            for sem in counters:
                sp.sem_inc(sem, per_layer[id(sem)] - (2 if any(sem is f for f in bank_free[0:4]) else 0))
            for j in range(KD // 2):
                sp.dma_start(xin[:, :, j * 2 * P:(j + 1) * 2 * P],
                             x[0].rearrange("(t p) d -> p t d", p=P)[:, :, j * 2 * P:(j + 1) * 2 * P]).then_inc(x_in[j], 16)
            for l in layers(sp):
                for b, (name, i) in enumerate(BLOCKS):
                    if l == 0 and b == 2:
                        sp.dma_start(consts[:, :], cst).then_inc(c_in, 16)
                    s, last = STAGE[b], previous(b, STAGE)
                    sp.wait_ge(w_hi_made, val(w_hi_made, l, last + 1))
                    sp.wait_ge(w_lo_made, val(w_lo_made, l, last + 1))
                    dst = stage[:, s, :]
                    if name == "dv":
                        src = w_in[l].rearrange("(k p) m -> p k m", p=P)[:, 2 * i:2 * i + 2, OFF_DV:P_IN]
                        dst = dst.rearrange("p (k m) -> p k m", k=2)
                    elif name == "uq":
                        src = w_uq[l][i * P:(i + 1) * P, :]
                        dst = stage[:, s, 0:MLA_HEADS * QK]
                    elif name == "ukv":
                        src = w_ukv[l][i * P:(i + 1) * P, :]
                    elif name == "kr":
                        src = w_in[l].rearrange("(k p) m -> p k m", p=P)[:, :, OFF_KR:OFF_DQ]
                        dst = stage[:, s, 0:KD * ROPE].rearrange("p (k m) -> p k m", k=KD)
                    elif name in ("outd", "outm"):
                        k0 = KD // 2 if name == "outd" else 0
                        src = w_out[l].rearrange("(k p) m -> p k m", p=P)[:, k0:k0 + TT, i * 256:(i + 1) * 256]
                        dst = dst.rearrange("p (k m) -> p k m", k=TT)
                    elif name.startswith("down"):
                        c = int(name[4:])
                        src = w_down[l].rearrange("(k p) m -> p k m", p=P)[:, c * FC:(c + 1) * FC, i * 256:(i + 1) * 256]
                        dst = dst.rearrange("p (k m) -> p k m", k=FC)
                    else:
                        if name.startswith("up"):
                            w, c0 = w_up, (int(name[2:]) * FC + i) * P
                        else:
                            base = {"cq": OFF_CQ, "ckv": OFF_CKV, "dk": OFF_DK, "dq": OFF_DQ}[name[:-1]]
                            w, c0 = w_in, base + int(name[-1]) * P
                        src = w[l].rearrange("(k p) m -> p k m", p=P)[:, :, c0:c0 + P]
                        dst = dst.rearrange("p (k m) -> p k m", k=KD)
                    sp.dma_start(dst, src).then_inc(stage_full[s], 16)
            for tt in range(TT):
                sp.wait_ge(y_left, tt + 1)
                sp.wait_ge(y_right, tt + 1)
                sp.dma_start(out[0, tt * P:(tt + 1) * P, :], yout[:, tt, :]).then_inc(y_out, 16)
            sp.wait_ge(y_out, 16 * TT)

        @block.gpsimd
        def _(pool):
            nc.gpsimd.memset(ident[:, :], 0.0).then_inc(consts_made, 1)
            nc.gpsimd.memset(ones[:, :], 1.0).then_inc(consts_made, 1)
            nc.gpsimd.memset(mhalf[:, :], -0.5).then_inc(consts_made, 1)
            pool.wait_ge(consts_made, 3)
            nc.gpsimd.affine_select(out=ident[:, :], in_=ident[:, :], compare_op=ALU.not_equal, fill=1.0,
                                    base=0, pattern=[[-1, P]], channel_multiplier=1).then_inc(consts_made, 1)

            for side, (a, b) in enumerate(((lam_q1, lam_q2), (lam_k1, lam_k2))):
                pool.dma_start(lam_r[0:2, side, :], a).then_inc(lam_in, 16)
                pool.dma_start(lam_r[2:4, side, :], b).then_inc(lam_in, 16)

            def power(l, m, k, dst):
                pool.wait_ge(misc_free, val(misc_free, l, m + 1))
                nc.gpsimd.tensor_tensor(dst[:, :], rc[:, :], mhalf[:, :], ALU.pow).then_inc(pow_done, 1)

            for l in layers(pool):
                power(l, MISC_AT["mix_c"], 0, rs_mix)
                power(l, MISC_AT["q_c"], 1, rs)
                power(l, MISC_AT["kv_c"], 2, rs)
                for g in range(DIFF_HEADS):
                    power(l, MISC_AT[f"sub{g}_c"], 3 + g, rs)
                power(l, MISC_AT["mlp_c"], 3 + DIFF_HEADS, rs)
            power(DEPTH, 0, 0, rs)

        @block.scalar
        def _(act):
            for w, r0, n in ((g_mix, G_MIX, DEPTH * KD), (g_mlp, G_MLP, DEPTH * KD), (g_q, G_Q, DEPTH * KC),
                             (g_kv, G_KV, DEPTH * KC), (g_sub, G_SUB, DEPTH)):
                act.dma_start(g_rows[r0:r0 + n, :], w.rearrange("l (t p) -> (l t) p", p=P)).then_inc(g_in, 16)
            act.dma_start(g_rows[G_FINAL:G_FINAL + KD, :], g_final.rearrange("(t p) -> t p", p=P)).then_inc(g_in, 16)
            def split(l, b):
                s, r = SLOT[b], STAGE[b]
                act.wait_ge(*staged(l, b))
                act.wait_ge(*block_used(l, previous(b)))
                hi, st, parts = block_parts(b)
                for d, f, n in parts:
                    last = nc.scalar.activation(hi(w_hi, s)[:, :, d:d + n], st(r)[:, :, f:f + n], ACT.Copy)
                last.then_inc(w_hi_made, 1)

            def square(l, n, src):
                act.wait_ge(ss_acc, val(ss_acc, l, n - 1))
                nc.scalar.activation(tmp_s[:, n % 2, :], src, ACT.Square).then_inc(sq_ready, 1)

            def exp_diff(l, e):
                act.wait_ge(sc_free, val(sc_free, l, e + 1))
                t = e % 6
                nc.scalar.activation(e_slot(t), e_slot(t), ACT.Exp, scale=-1.0, bias=nmx[:, t:t + 1],
                                     accum_out=rsum[:, t:t + 1]).then_inc(e_ready, 1)

            def t1(l, i):
                act.wait_ge(coef_ready, val(coef_ready, l, i + 1))
                t = 2 * (i % 3) + 1
                nc.scalar.activation(e_slot(t), e_slot(t), ACT.Copy, scale=coefs[:, t:t + 1]).then_inc(t1_ready, 1)

            def normalise(l, i):
                act.wait_ge(coef_ready, val(coef_ready, l, DSTEPS + i + 1))
                t = p_slot(i)
                nc.scalar.activation(e_t[:, t, :], e_t[:, t, :], ACT.Copy, scale=coefs[:, t:t + 1]
                                     ).then_inc(p_ready, 1)

            def exp_mla(l, i):
                act.wait_ge(mx_ready, val(mx_ready, l, i + 1))
                act.wait_ge(tr_done, val(tr_done, l, DSTEPS + i - 3))
                if i < 4:
                    act.wait_ge(tr_done, val(tr_done, l, DSTEPS - 2 if i < 2 else DSTEPS))
                e = 2 * DSTEPS + i
                t = p_slot(i)
                nc.scalar.activation(e_t[:, t, :], SC_BANKS[e % 3][:, :], ACT.Exp, bias=nmx[:, t:t + 1],
                                     accum_out=rsum[:, t:t + 1]).then_inc(sc_free, 1)

            def hi_pt(l, n):
                act.wait_ge(tr_done, val(tr_done, l, n + 1))
                if n % TT == 0:
                    g = n // TT
                    act.wait_ge(misc_done, val(misc_done, l, MISC_AT[f"pv{g - 1}"] + 1 if g else 0))
                q = n % TT
                nc.scalar.activation(pt_hi[:, :, q * P:(q + 1) * P], TR_BANKS[n % 2].rearrange("p (k c) -> p k c", k=TT),
                                     ACT.Copy).then_inc(pt_hi_made, 1)

            def gen(l, use):
                if use[0] == "d":
                    i = HEAD_USES.index(use)
                    act.wait_ge(*read_out(l, use))
                    nc.scalar.activation(dq_hi[:, i // 2, :] if i % 2 else d_keys(i // 2)[0], tmp_y[:, i % 2, :], ACT.Copy
                                         ).then_inc(d_hi_made, 1)
                    split(l, BLOCK_AT[(use, 0)] + RING)
                elif use[0] == "v":
                    tt = int(use[1:])
                    act.wait_ge(proj_done, val(proj_done, l, USE[use] + 1))
                    nc.scalar.activation(v_pack[:, tt, :, 0, :], bank[BANK[use]].rearrange("p (h c) -> p h c", h=MLA_HEADS),
                                         ACT.Copy).then_inc(v_hi_made, 1)
                elif use[0] == "k":
                    j = int(use[2:])
                    act.wait_ge(proj_done, val(proj_done, l, USE[use] + 1))
                    act.wait_ge(sc_done, val(sc_done, l, 2 * DSTEPS + TT * (2 * j - 2) if j else 2 * (DSTEPS - TT)))
                    if j == 1:
                        act.wait_ge(misc_done, val(misc_done, l, MISC_AT[f"pv{DIFF_HEADS - 1}"] + 1))
                    for p in range(2):
                        nc.scalar.activation(k_pack[0:NOPE, 2 * (j % 2) + p, 0, :],
                                             bank[BANK[use]][p * NOPE:(p + 1) * NOPE, :], ACT.Copy
                                             ).then_inc(k_hi_made, 1)
                elif use[0] == "q":
                    hd = int(use[1:])
                    act.wait_ge(qf_ready, val(qf_ready, l, hd + 1))
                    act.wait_ge(sc_done, val(sc_done, l, 2 * DSTEPS + TT * (hd - 1) if hd else 2 * (DSTEPS - TT)))
                    nc.scalar.activation(q_tile(hd)[0], tmp_y[0:QK, 0, :], ACT.Copy).then_inc(q_hi_made, 1)

            def pv_out(l, g):
                act.wait_ge(misc_done, val(misc_done, l, MISC_AT[f"pv{g}"] + 1))
                if g < DIFF_HEADS:
                    act.wait_ge(o_lo_made, val(o_lo_made, l, g))
                    nc.scalar.activation(tmp_s[:, 0, :], MISC_BANK[:, :], ACT.Copy)
                    nc.scalar.activation(tmp_s[:, 1, :], MISC_BANK[:, :], ACT.Square).then_inc(misc_free, 1)
                else:
                    act.wait_ge(misc_free, val(misc_free, l, MISC_AT[f"pv{g}"]))
                    nc.scalar.activation(tmp_s[0:MLA_V, 1, :], MISC_BANK[MLA_V:P, :], ACT.Copy).then_inc(o_half, 1)

            def o_split(l, n, t):
                if n < DIFF_HEADS:
                    act.wait_ge(misc_free, val(misc_free, l, MISC_AT[f"sub{n}_b"] + 1))
                else:
                    act.wait_ge(misc_free, val(misc_free, l, MISC_AT[f"pv{2 * n - DIFF_HEADS + 1}"] + 1))
                nc.scalar.activation(t[0], tmp_s[:, 0, :], ACT.Copy).then_inc(o_hi_made, 1)

            for j in range(1, KD, 2):
                act.wait_ge(xt_done, j + 1)
                nc.scalar.activation(h[:, j, :], bank[j % 4][:, :], ACT.Copy).then_inc(bank_free[j % 4], 1)
            for b in range(2):
                split(0, b)
            act.wait_ge(gt_copied, 1)

            def stream(l, j):
                act.wait_ge(*stream_ready(l, j))
                if l == DEPTH:
                    square(l, j, h[:, j, :])
                    nc.scalar.activation(gh[:, j, :], h[:, j, :], ACT.Copy, scale=g_cols[:, G_FINAL + j:G_FINAL + j + 1]
                                         ).then_inc(gh_made, 1)
                    return
                if j == 0:
                    act.wait_ge(proj_done, val(proj_done, l - 1, USE[f"up{CHUNKS - 1}_{FC - 1}"] + 1))
                nc.scalar.activation(u_hi[:, j, :], h[:, j, :], ACT.Copy, scale=cols(g_cols, G_MIX + j, l, KD)
                                     ).then_inc(u_hi_made, 1)
                square(l, j, h[:, j, :])

            for j in range(KD):
                stream(0, j)
            for l in layers(act):
                if l == 0:
                    for b in range(2, RING):
                        split(0, b)
                    act.wait_ge(lam_e, 1)
                    nc.scalar.activation(lam_s[:, 1:2], lam_s[:, 0:1], ACT.Exp).then_inc(lam_e, 1)
                for k, use in enumerate(LATENT_USES):
                    split(l, k + RING)
                    if use == "kr":
                        act.wait_ge(proj_done, val(proj_done, l, USE[use] + 1))
                        nc.scalar.activation(krf[0:2 * ROPE, :], bank[BANK[use]][2 * ROPE:4 * ROPE, :], ACT.Copy
                                             ).then_inc(kr_half, 1)
                    elif use != "ckv1":
                        act.wait_ge(*read_out(l, use))
                        square(l, KD + k, e_t[:, k, :])
                for b in range(TT):
                    split(l, BLOCK_AT[("dv", b)] + RING)
                    if b == 0:
                        act.wait_ge(*read_out(l, "ckv1"))
                        square(l, KD + 3, e_t[:, 3, :])
                    if b in (2, 3):
                        for i in (0, 1) if b == 2 else (2, 3):
                            act.wait_ge(c_ready, val(c_ready, l, i + 1))
                            nc.scalar.activation(c_hi[:, i, :], e_t[:, i, :], ACT.Copy).then_inc(c_hi_made, 1)
                for tt in range(TT):
                    act.wait_ge(dv_done, val(dv_done, l, TT))
                    nc.scalar.activation(dv_hi[:, tt, :], DV_BANKS[tt][:, :], ACT.Copy, scale=rs_mix[:, tt:tt + 1]
                                         ).then_inc(dv_hi_made, 1)
                for use in FIRST_USES:
                    gen(l, use)
                for n in range(STEPS + 5):
                    read_pt, pt_first = 3 <= n < STEPS + 3, n <= DSTEPS + 2 and (n - 3) % TT == TT - 1
                    if read_pt and pt_first:
                        hi_pt(l, n - 3)
                    if 0 < n <= DSTEPS:
                        t1(l, n - 1)
                    if read_pt and not pt_first:
                        hi_pt(l, n - 3)
                    if DSTEPS < n <= STEPS:
                        normalise(l, n - 1 - DSTEPS)
                    if n < DSTEPS:
                        exp_diff(l, 2 * n)
                        exp_diff(l, 2 * n + 1)
                    elif n < STEPS:
                        exp_mla(l, n - DSTEPS)
                    g, r = divmod(n - 7, TT)
                    if r == 0 and 0 <= g < DIFF_HEADS + MLA_HEADS:
                        pv_out(l, g)
                    if n in (DSTEPS - 4, DSTEPS + 3):
                        for p in (0, 1) if n == DSTEPS - 4 else (2, 3):
                            act.wait_ge(kr_ready, val(kr_ready, l, 1))
                            act.wait_ge(sc_done, val(sc_done, l, 2 * (DSTEPS - TT)))
                            if p >= 2:
                                act.wait_ge(misc_done, val(misc_done, l, MISC_AT[f"pv{DIFF_HEADS - 1}"] + 1))
                            nc.scalar.activation(k_pack[NOPE:QK, p, 0, :], krf[NOPE:QK, :], ACT.Copy
                                                 ).then_inc(krb_hi_made, 1)
                            if p:
                                act.wait_ge(krb_lo_made, val(krb_lo_made, l, 1))
                                nc.scalar.activation(k_pack[NOPE:QK, p, 1, :], k_pack[NOPE:QK, 0, 1, :].bitcast(F32),
                                                     ACT.Copy).then_inc(krb_copied, 1)
                    for use in ended(n - 1):
                        gen(l, use)
                    if r == 3 and 0 <= g < DIFF_HEADS:
                        o_split(l, g, o_tile(g))
                    if r == 2 and g >= DIFF_HEADS and (g - DIFF_HEADS) % 2 == 1:
                        hd = g - DIFF_HEADS
                        if hd < MLA_HEADS:
                            o_split(l, DIFF_HEADS + hd // 2, o_tile(DIFF_HEADS + hd // 2))
                    if n in OUT_SPLITS:
                        split(l, OUT_SPLITS[n])
                o_split(l, KD - 1, o_tile(KD - 1))
                for k, j in enumerate(HALVES):
                    if k % 2:
                        split(l, OUTM_AT + k // 2 + RING)
                    act.wait_ge(*read_out(l, f"outm{j}"))
                    if k >= KD // 2:
                        square(l, KD + 2 * KC + k - KD // 2, h[:, HALVES[k - KD // 2], :])
                    else:
                        nc.scalar.activation(u_hi[:, j, :], h[:, j, :], ACT.Copy, scale=cols(g_cols, G_MLP + j, l, KD)
                                             ).then_inc(u_hi_made, 1)
                for j in HALVES[KD // 2:]:
                    act.wait_ge(proj_done, val(proj_done, l, USE[OUTM_USES[-1]] + 1))
                    nc.scalar.activation(u_hi[:, j, :], h[:, j, :], ACT.Copy, scale=cols(g_cols, G_MLP + j, l, KD)
                                         ).then_inc(u_hi_made, 1)
                for k in range(KD // 2, KD):
                    square(l, KD + 2 * KC + k, h[:, HALVES[k], :])
                b = BLOCK_AT[("up0", 0)]
                f = 0
                for kind, c in mlp_order():
                    for i in range(FC):
                        if b + RING < NBLK:
                            split(l, b + RING)
                        elif l + 1 < DEPTH:
                            split(l + 1, b + RING - NBLK)
                        b += 1
                        if kind == "up":
                            act.wait_ge(hid_f, val(hid_f, l, f + 1))
                            if i == 0:
                                if c >= 2:
                                    act.wait_ge(proj_done, val(proj_done, l, USE[f"down{c - 2}_{KD - 1}"] + 1))
                            nc.scalar.activation(hid_hi[:, c % 2, i, :], tmp_y[:, 1, :], ACT.Copy).then_inc(hid_hi_made, 1)
                            f += 1
                        elif c == CHUNKS - 1:
                            stream(l + 1, 2 * i)
                            stream(l + 1, 2 * i + 1)
            act.wait_ge(pow_done, val(pow_done, DEPTH, 1))
            for tt in range(TT):
                act.wait_ge(yt_done, tt + 1)
                nc.scalar.activation(yout[:, tt, D_MODEL // 2:], Y_BANKS[1][tt][:, :], ACT.Copy, scale=rs[:, tt:tt + 1]
                                     ).then_inc(y_right, 1)

        @block.vector
        def _(dve):
            chain = [0]

            def link(l, ins):
                chain[0] += 1
                ins.then_inc(chain_done, 1)
                dve.wait_ge(chain_done, val(chain_done, l, chain[0]))

            def split(l, b):
                s, r = SLOT[b], STAGE[b]
                dve.wait_ge(w_hi_made, val(w_hi_made, l, b + 1))
                if BLOCKS[b][0] == "kr":
                    dve.wait_ge(*block_used(l, previous(b)))
                hi, st, parts = block_parts(b)
                for d, f, n in parts:
                    dst = (hi(w_hi, s)[:, :, 2 * ROPE + d:2 * ROPE + d + n] if BLOCKS[b][0] == "kr"
                           else hi(w_lo, s)[:, :, d:d + n])
                    last = nc.vector.tensor_tensor(dst, st(r)[:, :, f:f + n],
                                                   hi(w_hi, s)[:, :, d:d + n].bitcast(F32), ALU.subtract)
                last.then_inc(w_lo_made, 1)

            def add_square(l, n, first):
                dve.wait_ge(sq_ready, val(sq_ready, l, n + 1))
                if first:
                    nc.vector.tensor_copy(ss[:, :], tmp_s[:, n % 2, :]).then_inc(ss_acc, 1)
                else:
                    dve.wait_ge(ss_acc, val(ss_acc, l, n))
                    nc.vector.tensor_tensor(ss[:, :], ss[:, :], tmp_s[:, n % 2, :], ALU.add).then_inc(ss_acc, 1)

            def stat_col(l, m, count, eps):
                dve.wait_ge(misc_done, val(misc_done, l, m + 1))
                nc.vector.tensor_scalar(rc[:, :], MISC_BANK[:, 0:TT], 1.0 / count, eps, ALU.mult, ALU.add
                                        ).then_inc(misc_free, 1)

            def stat_diag(l, k, src):
                dve.wait_ge(pow_done, val(pow_done, l, k + 1))
                for tt in range(TT):
                    last = nc.vector.tensor_scalar(diag[:, tt, :], ident[:, :], src[:, tt:tt + 1], None, ALU.mult)
                last.then_inc(diag_ready, 1)

            def stat_row(l, m, dst):
                dve.wait_ge(misc_done, val(misc_done, l, m + 1))
                nc.vector.tensor_copy(dst, MISC_BANK[:, :]).then_inc(misc_free, 1)
                dve.wait_ge(misc_free, val(misc_free, l, m + 1))

            def ttr(l, e):
                i, m = divmod(e, 2)
                hd, qt = divmod(i, TT)
                dve.wait_ge(sc_done, val(sc_done, l, e + 1))
                dve.wait_ge(tr_done, val(tr_done, l, i - 2 if i >= 3 else 0))
                off = C_NEGD + (TT - 1 - qt) * P
                nc.vector.tensor_tensor_reduce(e_slot(e % 6), SC_BANKS[e % 3][:, :], consts[:, off:off + SEQ],
                                               -SLOPES[hd], 3.0e38, ALU.add, ALU.min, nmx[:, e % 6:e % 6 + 1]
                                               ).then_inc(sc_free, 1)

            def coef(l, i):
                t = 2 * (i % 3)
                dve.wait_ge(e_ready, val(e_ready, l, 2 * i + 2))
                link(l, nc.vector.reciprocal(coefs[:, t:t + 2], rsum[:, t:t + 2]))
                nc.vector.tensor_scalar(coefs[:, t + 1:t + 2], coefs[:, t + 1:t + 2], cols(lam_b, 0, l), None, ALU.mult
                                        ).then_inc(coef_ready, 1)

            def weights(l, i):
                t = 2 * (i % 3)
                dve.wait_ge(t1_ready, val(t1_ready, l, i + 1))
                nc.vector.scalar_tensor_tensor(out=e_slot(t), in0=e_slot(t), scalar=coefs[:, t:t + 1],
                                               in1=e_slot(t + 1), op0=ALU.mult, op1=ALU.subtract
                                               ).then_inc(w_ready, 1)

            def row_max(l, i):
                e = 2 * DSTEPS + i
                dve.wait_ge(sc_done, val(sc_done, l, e + 1))
                nc.vector.tensor_reduce(nmx[:, p_slot(i):p_slot(i) + 1], SC_BANKS[e % 3][:, :], AX_X, ALU.max, negate=True
                                        ).then_inc(mx_ready, 1)

            def inverse_sum(l, i):
                dve.wait_ge(sc_free, val(sc_free, l, 2 * DSTEPS + i + 1))
                t = p_slot(i)
                nc.vector.reciprocal(coefs[:, t:t + 1], rsum[:, t:t + 1]).then_inc(coef_ready, 1)

            def lo_pt(l, n):
                q = n % TT
                dve.wait_ge(pt_hi_made, val(pt_hi_made, l, n + 1))
                piece = lambda t: t[:, :, q * P:(q + 1) * P]
                nc.vector.tensor_tensor(piece(pt_lo), TR_BANKS[n % 2].rearrange("p (k c) -> p k c", k=TT),
                                        piece(pt_hi).bitcast(F32), ALU.subtract).then_inc(pt_lo_made, 1)

            def gen(l, use):
                b = bank[BANK[use]]
                dve.wait_ge(proj_done, val(proj_done, l, USE[use] + 1))
                if use[0] == "d":
                    i = HEAD_USES.index(use)
                    dve.wait_ge(d_lo_made, val(d_lo_made, l, max(0, i - 1)))
                    if i % 2 == 0:
                        nc.vector.tensor_tensor(tmp_y[:, 0, :], b[:, :], rb[:, :], ALU.mult).then_inc(freed(use), 1)
                    else:
                        c = DIFF_D ** -0.5 / SLOPES[i // 2]
                        nc.vector.scalar_tensor_tensor(out=tmp_y[:, 1, :], in0=b[:, :], scalar=c, in1=rb[:, :],
                                                       op0=ALU.mult, op1=ALU.mult).then_inc(freed(use), 1)
                elif use[0] == "o":
                    j = int(use[4:])
                    dve.wait_ge(sq_ready, val(sq_ready, l, j + 1))
                    nc.vector.tensor_tensor(h[:, j, :], h[:, j, :], b[:, :], ALU.add).then_inc(freed(use), 1)
                elif use[0] == "q":
                    dve.wait_ge(d_lo_made, val(d_lo_made, l, 2 * DIFF_HEADS))
                    dve.wait_ge(q_lo_made, val(q_lo_made, l, int(use[1:])))
                    nc.vector.tensor_tensor(tmp_y[0:QK, 0, :], b[0:QK, :], tabq[0:QK, :], ALU.mult)
                    nc.vector.tensor_tensor(tmp_y[NOPE:QK, 1, :], b[QK:P, :], tabq[QK:P, :], ALU.mult
                                            ).then_inc(freed(use), 1)
                    dve.wait_ge(*read_out(l, use))
                    nc.vector.tensor_tensor(tmp_y[NOPE:QK, 0, :], tmp_y[NOPE:QK, 0, :], tmp_y[NOPE:QK, 1, :], ALU.add
                                            ).then_inc(qf_ready, 1)

            def gen_low(l, use):
                b = bank[BANK[use]]
                if use[0] == "d":
                    i = HEAD_USES.index(use)
                    hi, lo = (dq_hi[:, i // 2, :], dq_lo[:, i // 2, :]) if i % 2 else d_keys(i // 2)
                    dve.wait_ge(d_hi_made, val(d_hi_made, l, i + 1))
                    nc.vector.tensor_tensor(lo, tmp_y[:, i % 2, :], hi.bitcast(F32), ALU.subtract).then_inc(d_lo_made, 1)
                    split(l, BLOCK_AT[(use, 0)] + RING)
                elif use[0] == "v":
                    tt = int(use[1:])
                    dve.wait_ge(v_hi_made, val(v_hi_made, l, tt + 1))
                    nc.vector.tensor_tensor(v_pack[:, tt, :, 1, :], b.rearrange("p (h c) -> p h c", h=MLA_HEADS),
                                            v_pack[:, tt, :, 0, :].bitcast(F32), ALU.subtract).then_inc(freed(use), 1)
                elif use[0] == "k":
                    j = int(use[2:])
                    for p in range(2):
                        dve.wait_ge(k_hi_made, val(k_hi_made, l, 2 * j + p + 1))
                        s = 2 * (j % 2) + p
                        last = nc.vector.tensor_tensor(k_pack[0:NOPE, s, 1, :], b[p * NOPE:(p + 1) * NOPE, :],
                                                       k_pack[0:NOPE, s, 0, :].bitcast(F32), ALU.subtract)
                    last.then_inc(freed(use), 1)
                elif use[0] == "q":
                    hd = int(use[1:])
                    dve.wait_ge(q_hi_made, val(q_hi_made, l, hd + 1))
                    nc.vector.tensor_tensor(q_tile(hd)[1], tmp_y[0:QK, 0, :], q_tile(hd)[0].bitcast(F32), ALU.subtract
                                            ).then_inc(q_lo_made, 1)

            def o_low(l, n, t):
                dve.wait_ge(o_hi_made, val(o_hi_made, l, n + 1))
                nc.vector.tensor_tensor(t[1], tmp_s[:, 0, :], t[0].bitcast(F32), ALU.subtract
                                        ).then_inc(o_lo_made, 1)

            def pv_out(l, g):
                hd = g - DIFF_HEADS
                p = (hd % 2) * MLA_V
                dve.wait_ge(o_half, val(o_half, l, hd + 1))
                dve.wait_ge(o_lo_made, val(o_lo_made, l, DIFF_HEADS + hd // 2))
                nc.vector.tensor_tensor(tmp_s[p:p + MLA_V, 0, :], MISC_BANK[0:MLA_V, :], tmp_s[0:MLA_V, 1, :], ALU.add
                                        ).then_inc(misc_free, 1)

            def stream_low(l, k, j):
                dve.wait_ge(u_hi_made, val(u_hi_made, l, KD + k + 1))
                nc.vector.scalar_tensor_tensor(out=u_low(j), in0=h[:, j, :], scalar=cols(g_cols, G_MLP + j, l, KD),
                                               in1=u_hi[:, j, :].bitcast(F32), op0=ALU.mult, op1=ALU.subtract
                                               ).then_inc(u_lo_made, 1)

            for j in range(0, KD, 2):
                dve.wait_ge(xt_done, j + 1)
                nc.vector.tensor_copy(h[:, j, :], bank[j % 4][:, :]).then_inc(bank_free[j % 4], 1)
                if j == 0:
                    dve.wait_ge(gt_done, 1)
                    nc.vector.tensor_copy(g_cols[:, :], bank[6][:, 0:G_ROWS]).then_inc(gt_copied, 1)
            dve.wait_ge(lam_in, 64)
            nc.vector.tensor_tensor_reduce(lam_r[:, 0, :], lam_r[:, 0, :], lam_r[:, 1, :], 1.0, 0.0, ALU.mult, ALU.add,
                                           lam_s[:, 0:1]).then_inc(lam_e, 1)
            for b in range(2):
                split(0, b)

            def stream(l, j):
                if l < DEPTH:
                    dve.wait_ge(u_hi_made, val(u_hi_made, l, j + 1))
                    nc.vector.scalar_tensor_tensor(out=u_low(j), in0=h[:, j, :], scalar=cols(g_cols, G_MIX + j, l, KD),
                                                   in1=u_hi[:, j, :].bitcast(F32), op0=ALU.mult, op1=ALU.subtract
                                                   ).then_inc(u_lo_made, 1)
                add_square(l, j, j == 0)

            for j in range(KD):
                stream(0, j)
            for l in layers(dve):
                chain[0] = 0
                if l == 0:
                    for b in range(2, RING):
                        split(0, b)
                stat_col(l, MISC_AT["mix_c"], D_MODEL, EPS)
                stat_diag(l, 0, rs_mix)
                stat_row(l, MISC_AT["mix_b"], rb[:, :])
                for k, use in enumerate(LATENT_USES):
                    b = bank[BANK[use]]
                    dve.wait_ge(proj_done, val(proj_done, l, USE[use] + 1))
                    if use != "kr":
                        nc.vector.tensor_tensor(e_t[:, k, :], b[:, :], rb[:, :], ALU.mult).then_inc(freed(use), 1)
                        if use == "cq1":
                            add_square(l, KD, True)
                            add_square(l, KD + 1, False)
                    else:
                        if l == 0:
                            dve.wait_ge(c_in, 16)
                            dve.wait_ge(lam_e, 2)
                            nc.vector.tensor_scalar(lam_s[:, 2:2 + DEPTH], sign, lam_s[:, 1:2], None, ALU.mult
                                                    ).then_inc(lam_m, 1)
                        link(l, nc.vector.tensor_tensor(ck[0:2 * ROPE, :], tabk[0:2 * ROPE, :], rb[0:2 * ROPE, :], ALU.mult))
                        dve.wait_ge(kr_half, val(kr_half, l, 1))
                        nc.vector.tensor_tensor(krf[0:2 * ROPE, :], b[0:2 * ROPE, :], krf[0:2 * ROPE, :], ALU.add
                                                ).then_inc(freed(use), 1)
                        dve.wait_ge(*read_out(l, use))
                        link(l, nc.vector.tensor_tensor(krf[0:2 * ROPE, :], krf[0:2 * ROPE, :], ck[0:2 * ROPE, :], ALU.mult))
                        link(l, nc.vector.tensor_copy(ck[0:ROPE, :], krf[ROPE:2 * ROPE, :]))
                        nc.vector.tensor_tensor(krf[NOPE:QK, :], krf[0:ROPE, :], ck[0:ROPE, :], ALU.add
                                                ).then_inc(kr_ready, 1)
                    split(l, k + RING)
                for b in range(TT):
                    split(l, BLOCK_AT[("dv", b)] + RING)
                    if b == 0:
                        stat_col(l, MISC_AT["q_c"], LORA, EPS)
                        add_square(l, KD + 2, True)
                        add_square(l, KD + 3, False)
                        stat_diag(l, 1, rs)
                    if b == 1:
                        stat_row(l, MISC_AT["q_b"], rb_c[:, :])
                        for t in range(KC):
                            nc.vector.scalar_tensor_tensor(out=e_t[:, t, :], in0=e_t[:, t, :],
                                                           scalar=cols(g_cols, G_Q + t, l, KC), in1=rb_c[:, :],
                                                           op0=ALU.mult, op1=ALU.mult).then_inc(c_ready, 1)
                    if b == 2:
                        stat_col(l, MISC_AT["kv_c"], LORA, EPS)
                        for t in range(KC):
                            dve.wait_ge(c_hi_made, val(c_hi_made, l, t + 1))
                            nc.vector.tensor_tensor(c_lo[:, t, :], e_t[:, t, :], c_hi[:, t, :].bitcast(F32), ALU.subtract
                                                    ).then_inc(c_lo_made, 1)
                        stat_diag(l, 2, rs)
                stat_row(l, MISC_AT["kv_b"], rb_c[:, :])
                for t in range(KC, 2 * KC):
                    nc.vector.scalar_tensor_tensor(out=e_t[:, t, :], in0=e_t[:, t, :],
                                                   scalar=cols(g_cols, G_KV + t - KC, l, KC), in1=rb_c[:, :],
                                                   op0=ALU.mult, op1=ALU.mult).then_inc(c_ready, 1)
                for t in range(KC, 2 * KC):
                    dve.wait_ge(c_hi_made, val(c_hi_made, l, t + 1))
                    nc.vector.tensor_tensor(c_lo[:, t, :], e_t[:, t, :], c_hi[:, t, :].bitcast(F32), ALU.subtract
                                            ).then_inc(c_lo_made, 1)
                for tt in range(TT):
                    dve.wait_ge(dv_hi_made, val(dv_hi_made, l, tt + 1))
                    nc.vector.scalar_tensor_tensor(out=dv_lo[:, tt, :], in0=DV_BANKS[tt][:, :], scalar=rs_mix[:, tt:tt + 1],
                                                   in1=dv_hi[:, tt, :].bitcast(F32), op0=ALU.mult, op1=ALU.subtract
                                                   ).then_inc(dv_lo_made, 1)
                for use in FIRST_USES:
                    gen(l, use)
                    gen_low(l, use)
                if l == 0:
                    dve.wait_ge(lam_m, 2)
                    nc.vector.tensor_tensor(lam_b[:, :], bank[7][:, 0:DEPTH], consts[:, C_INIT:C_INIT + DEPTH], ALU.add
                                            ).then_inc(lam_done, 1)
                    nc.vector.tensor_tensor(gsl[:, :], g_cols[:, G_SUB:G_SUB + DEPTH], consts[:, C_GSC:C_GSC + DEPTH], ALU.mult
                                            ).then_inc(lam_done, 1)
                    dve.wait_ge(lam_done, 2)
                for n in range(STEPS + 5):
                    read_pt, pt_first = 3 <= n < STEPS + 3, n <= DSTEPS + 2 and (n - 3) % TT == TT - 1
                    if read_pt and pt_first:
                        lo_pt(l, n - 3)
                    if 0 < n <= DSTEPS:
                        coef(l, n - 1)
                    if n < DSTEPS:
                        ttr(l, 2 * n)
                        ttr(l, 2 * n + 1)
                    elif n == DSTEPS:
                        weights(l, n - 1)
                        row_max(l, 0)
                    elif n <= STEPS:
                        inverse_sum(l, n - 1 - DSTEPS)
                        if n < STEPS:
                            row_max(l, n - DSTEPS)
                    g, r = divmod(n - 8, TT)
                    if r == 0 and DIFF_HEADS <= g < DIFF_HEADS + MLA_HEADS - 1:
                        pv_out(l, g)
                    if 0 < n < DSTEPS:
                        weights(l, n - 1)
                    if read_pt and not pt_first:
                        lo_pt(l, n - 3)
                    if r == 2 and 0 <= g < DIFF_HEADS:
                        dve.wait_ge(misc_done, val(misc_done, l, MISC_AT[f"sub{g}_b"] + 1))
                        nc.vector.scalar_tensor_tensor(out=tmp_s[:, 0, :], in0=tmp_s[:, 0, :], scalar=cols(gsl, 0, l),
                                                       in1=MISC_BANK[:, :], op0=ALU.mult, op1=ALU.mult
                                                       ).then_inc(misc_free, 1)
                    if r == 3 and 0 <= g < DIFF_HEADS:
                        o_low(l, g, o_tile(g))
                    if r == 0 and 0 <= g < DIFF_HEADS:
                        stat_col(l, MISC_AT[f"sub{g}_c"], 2 * DIFF_D, SUBLN_EPS)
                    if n == DSTEPS - 4:
                        dve.wait_ge(krb_hi_made, val(krb_hi_made, l, 1))
                        nc.vector.tensor_tensor(k_pack[NOPE:QK, 0, 1, :], krf[NOPE:QK, :],
                                                k_pack[NOPE:QK, 0, 0, :].bitcast(F32), ALU.subtract
                                                ).then_inc(krb_lo_made, 1)
                    for use in ended(n - 2):
                        if use[0] != "o":
                            gen_low(l, use)
                    for use in ended(n - 1):
                        if use[0] not in "vk":
                            gen(l, use)
                    if r == 0 and 0 <= g < DIFF_HEADS:
                        stat_diag(l, 3 + g, rs)
                    if r == 1 and g >= DIFF_HEADS and (g - DIFF_HEADS) % 2 == 1 and g < DIFF_HEADS + MLA_HEADS - 1:
                        hd = g - DIFF_HEADS
                        o_low(l, DIFF_HEADS + hd // 2, o_tile(DIFF_HEADS + hd // 2))
                    if n - 1 in OUT_SPLITS:
                        split(l, OUT_SPLITS[n - 1])
                pv_out(l, DIFF_HEADS + MLA_HEADS - 1)
                o_low(l, KD - 1, o_tile(KD - 1))
                for k, j in enumerate(HALVES):
                    use = f"outm{j}"
                    if k in (KD // 2, KD // 2 + 1):
                        for i in (0, 1) if k == KD // 2 else (2, 3):
                            stream_low(l, i, HALVES[i])
                    dve.wait_ge(proj_done, val(proj_done, l, USE[use] + 1))
                    nc.vector.tensor_tensor(h[:, j, :], h[:, j, :], bank[BANK[use]][:, :], ALU.add).then_inc(freed(use), 1)
                    if k % 2:
                        split(l, OUTM_AT + k // 2 + RING)
                    if k >= KD // 2:
                        add_square(l, KD + 2 * KC + k - KD // 2, k == KD // 2)
                for k in range(KD // 2, KD):
                    stream_low(l, k, HALVES[k])
                for k in range(KD // 2, KD):
                    add_square(l, KD + 2 * KC + k, False)
                stat_col(l, MISC_AT["mlp_c"], D_MODEL, EPS)
                stat_diag(l, 3 + DIFF_HEADS, rs)
                stat_row(l, MISC_AT["mlp_b"], rb[:, :])
                b = BLOCK_AT[("up0", 0)]
                f = 0
                for kind, c in mlp_order():
                    for i in range(FC):
                        if kind == "up":
                            use = f"up{c}_{i}"
                            dve.wait_ge(proj_done, val(proj_done, l, USE[use] + 1))
                            nc.vector.tensor_tensor(tmp_y[:, 0, :], bank[BANK[use]][:, :], rb[:, :], ALU.mult
                                                    ).then_inc(freed(use), 1)
                            dve.wait_ge(*read_out(l, use))
                            nc.vector.scalar_tensor_tensor(out=tmp_y[:, 1, :], in0=tmp_y[:, 0, :], scalar=0.0,
                                                           in1=tmp_y[:, 0, :], op0=ALU.max, op1=ALU.mult
                                                           ).then_inc(hid_f, 1)
                            f += 1
                        else:
                            for j in (2 * i, 2 * i + 1):
                                use = f"down{c}_{j}"
                                dve.wait_ge(proj_done, val(proj_done, l, USE[use] + 1))
                                nc.vector.tensor_tensor(h[:, j, :], h[:, j, :], bank[BANK[use]][:, :], ALU.add
                                                        ).then_inc(freed(use), 1)
                        if b + RING < NBLK:
                            split(l, b + RING)
                        elif l + 1 < DEPTH:
                            split(l + 1, b + RING - NBLK)
                        b += 1
                        if kind == "down" and c == CHUNKS - 1:
                            stream(l + 1, 2 * i)
                            stream(l + 1, 2 * i + 1)
                        if kind == "up":
                            dve.wait_ge(hid_hi_made, val(hid_hi_made, l, f))
                            nc.vector.tensor_tensor(hid_lo[:, c % 2, i, :], tmp_y[:, 1, :], hid_hi[:, c % 2, i, :].bitcast(F32),
                                                    ALU.subtract).then_inc(hid_lo_made, 1)
                assert chain[0] == CHAIN, chain[0]
            stat_col(DEPTH, 0, D_MODEL, EPS)
            dve.wait_ge(pow_done, val(pow_done, DEPTH, 1))
            for tt in range(TT):
                dve.wait_ge(yt_done, tt + 1)
                nc.vector.tensor_scalar(yout[:, tt, 0:D_MODEL // 2], Y_BANKS[0][tt][:, :], rs[:, tt:tt + 1], None, ALU.mult
                                        ).then_inc(y_left, 1)

        @block.tensor
        def _(pe):
            def three(acc, terms, first, last):
                for t, ((a_hi, a_lo), (b_hi, b_lo)) in enumerate(terms):
                    for m, (a, b) in enumerate(((a_hi, b_hi), (a_hi, b_lo), (a_lo, b_hi))):
                        mm = nc.tensor.matmul(acc, a, b, start=first and t == 0 and m == 0,
                                              stop=last and t == len(terms) - 1 and m == 2)
                return mm

            def wtile(s, k, w=P):
                return w_hi[:, s, k * w:(k + 1) * w], w_lo[:, s, k * w:(k + 1) * w]

            def u(k):
                return u_hi[:, k, :], u_low(k)

            def stat_c(l, m, src=None):
                pe.wait_ge(misc_free, val(misc_free, l, m))
                for tt in range(TT):
                    mm = nc.tensor.matmul(MISC_BANK[:, tt:tt + 1], (ss[:, tt * P:(tt + 1) * P] if src is None
                                                                   else src[:, tt * P:(tt + 1) * P]),
                                          ones[:, 0:1], start=True, stop=True)
                mm.then_inc(misc_done, 1)

            def stat_b(l, m, k):
                pe.wait_ge(diag_ready, val(diag_ready, l, k + 1))
                pe.wait_ge(misc_free, val(misc_free, l, m))
                nc.tensor.matmul(MISC_BANK[:, :], ones[:, :], diag.rearrange("p t c -> p (t c)"), start=True, stop=True
                                 ).then_inc(misc_done, 1)

            def scores_diff(l, n, m):
                hd, qt = divmod(n, TT)
                if qt == 0:
                    pe.wait_ge(d_lo_made, val(d_lo_made, l, 2 * hd + 2))
                e = 2 * n + m
                pe.wait_ge(sc_free, val(sc_free, l, e - 2))
                rows = slice(m * DIFF_D, (m + 1) * DIFF_D)
                three(SC_BANKS[e % 3][:, :],
                      [((dq_hi[rows, hd, qt * P:(qt + 1) * P], dq_lo[rows, hd, qt * P:(qt + 1) * P]),
                        tuple(k[rows, :] for k in d_keys(hd)))], True, True).then_inc(sc_done, 1)

            def scores(l, n):
                hd, qt = divmod(n - DSTEPS, TT)
                e = DSTEPS + n
                if qt == 0:
                    pe.wait_ge(q_lo_made, val(q_lo_made, l, hd + 1))
                    pe.wait_ge(krb_lo_made, val(krb_lo_made, l, 1))
                    pe.wait_ge(krb_copied, val(krb_copied, l, 1 if hd < 2 else 3))
                    pe.wait_ge(*read_out(l, f"kp{hd // 2}"))
                pe.wait_ge(sc_free, val(sc_free, l, e - 2))
                three(SC_BANKS[e % 3][:, :],
                      [(tuple(q[:, qt * P:(qt + 1) * P] for q in q_tile(hd)),
                        (k_pack[0:QK, hd % 4, 0, :], k_pack[0:QK, hd % 4, 1, :]))], True, True).then_inc(sc_done, 1)

            def turn(l, n):
                t = 2 * (n % 3) if n < DSTEPS else p_slot(n - DSTEPS)
                if n < DSTEPS:
                    pe.wait_ge(w_ready, val(w_ready, l, n + 1))
                else:
                    pe.wait_ge(p_ready, val(p_ready, l, n - DSTEPS + 1))
                pe.wait_ge(pt_lo_made, val(pt_lo_made, l, n - 1))
                for kt in range(TT):
                    mm = nc.tensor.transpose(TR_BANKS[n % 2][:, kt * P:(kt + 1) * P], e_slot(t)[:, kt * P:(kt + 1) * P],
                                             ident[:, :])
                mm.then_inc(tr_done, 1)

            def values(l, g):
                m = MISC_AT[f"pv{g}"]
                pe.wait_ge(pt_lo_made, val(pt_lo_made, l, TT * (g + 1)))
                pe.wait_ge(misc_free, val(misc_free, l, m))
                if g < DIFF_HEADS:
                    c = slice(g * 2 * DIFF_D, (g + 1) * 2 * DIFF_D)
                    three(MISC_BANK[:, :], [((dv_hi[:, kt, c], dv_lo[:, kt, c]), (pt_hi[:, kt, :], pt_lo[:, kt, :]))
                                            for kt in range(TT)], True, True).then_inc(misc_done, 1)
                    return
                hd = g - DIFF_HEADS
                if hd == 0:
                    for tt in range(TT):
                        pe.wait_ge(*read_out(l, f"v{tt}"))
                for kt in range(TT):
                    for pt in (pt_hi, pt_lo):
                        mm = nc.tensor.matmul(MISC_BANK[:, :], v_pack[:, kt, hd, :, :].rearrange("p a c -> p (a c)"),
                                              pt[:, kt, :], start=(kt == 0 and pt is pt_hi), stop=(kt == TT - 1 and pt is pt_lo))
                mm.then_inc(misc_done, 1)

            def block_ready(l, b):
                return (w_hi_made, val(w_hi_made, l, b + 1)), (w_lo_made, val(w_lo_made, l, b + 1))

            def head_sum(l, use, part):
                high, low = block_ready(l, BLOCK_AT[(use, 0)])
                pe.wait_ge(*high)
                pe.wait_ge(*low)
                pe.wait_ge(*taken(l, use))
                for t in part:
                    mm = three(bank[BANK[use]][:, :], [(wtile(SLOT[BLOCK_AT[(use, 0)]], t), u(t))], t == 0, t == KD - 1)
                if part[-1] == KD - 1:
                    mm.then_inc(proj_done, 1)

            def out_sum(l, use, part):
                j, name = int(use[4:]), use[:4]
                high, low = block_ready(l, BLOCK_AT[(name, j // 2)])
                pe.wait_ge(*high)
                pe.wait_ge(*low)
                pe.wait_ge(*taken(l, use))
                s = SLOT[BLOCK_AT[(name, j // 2)]]
                for t in part:
                    n = t if name == "outd" else DIFF_HEADS + t
                    pe.wait_ge(o_lo_made, val(o_lo_made, l, n + 1))
                    w = tuple(x[:, s, t * 256 + (j % 2) * P:t * 256 + (j % 2 + 1) * P] for x in (w_hi, w_lo))
                    mm = three(bank[BANK[use]][:, :], [(w, o_tile(n))], t == 0, t == TT - 1)
                if part[-1] == TT - 1:
                    mm.then_inc(proj_done, 1)

            def latent_sum(l, use):
                pe.wait_ge(*taken(l, use))
                acc = bank[BANK[use]][:, :]
                i = int(use.lstrip("vqkp"))
                terms = []
                for k in range(KC):
                    block_at = BLOCK_AT[("uq" if use[0] == "q" else "ukv", k)]
                    s = SLOT[block_at]
                    high, low = block_ready(l, block_at)
                    pe.wait_ge(*high)
                    pe.wait_ge(*low)
                    if use[0] == "q":
                        terms.append((wtile(s, i), (c_hi[:, k, :], c_lo[:, k, :])))
                        continue
                    wv = [t[:, s, :] for t in (w_hi, w_lo)]
                    if use[0] == "k":
                        terms.append((tuple(w[:, i * P:(i + 1) * P] for w in wv), (c_hi[:, KC + k, :], c_lo[:, KC + k, :])))
                    else:
                        terms.append((tuple(c[:, KC + k, i * P:(i + 1) * P] for c in (c_hi, c_lo)),
                                      tuple(w[:, MLA_HEADS * NOPE:] for w in wv)))
                three(acc, terms, True, True).then_inc(proj_done, 1)

            pe.wait_ge(consts_made, 4)
            pe.wait_ge(g_in, 96)
            nc.tensor.transpose(bank[6][:, 0:G_ROWS], g_rows[0:G_ROWS, :], ident[0:G_ROWS, 0:G_ROWS]).then_inc(gt_done, 1)
            for j in range(KD):
                pe.wait_ge(x_in[j // 2], 16)
                if j >= 4:
                    pe.wait_ge(bank_free[j % 4], val(bank_free[j % 4], -1, -1 + BANK_USES[j % 4]))
                for tt in range(TT):
                    mm = nc.tensor.transpose(bank[j % 4][:, tt * P:(tt + 1) * P], xin[:, tt, j * P:(j + 1) * P], ident[:, :])
                mm.then_inc(xt_done, 1)

            for l in layers(pe):
                for use in ("cq0", "cq1"):
                    pe.wait_ge(w_hi_made, val(w_hi_made, l, BLOCK_AT[(use, 0)] + 1))
                    pe.wait_ge(w_lo_made, val(w_lo_made, l, BLOCK_AT[(use, 0)] + 1))
                    pe.wait_ge(*taken(l, use))
                for t in range(KD):
                    pe.wait_ge(u_lo_made, val(u_lo_made, l, t + 1))
                    for use in ("cq0", "cq1"):
                        mm = three(bank[BANK[use]][:, :], [(wtile(SLOT[BLOCK_AT[(use, 0)]], t), u(t))], t == 0, t == KD - 1)
                        if t == KD - 1:
                            mm.then_inc(proj_done, 1)
                pe.wait_ge(ss_acc, val(ss_acc, l, KD))
                stat_c(l, MISC_AT["mix_c"])
                head_sum(l, "ckv0", range(KD))
                stat_b(l, MISC_AT["mix_b"], 0)
                head_sum(l, "ckv1", range(KD))
                pe.wait_ge(w_hi_made, val(w_hi_made, l, BLOCK_AT[("kr", 0)] + 1))
                pe.wait_ge(w_lo_made, val(w_lo_made, l, BLOCK_AT[("kr", 0)] + 1))
                pe.wait_ge(*taken(l, "kr"))
                for t in range(KD):
                    for m in range(2):
                        mm = nc.tensor.matmul(bank[BANK["kr"]][:, :], w_hi[:, SLOT[BLOCK_AT[("kr", 0)]], t * P:(t + 1) * P],
                                              u(t)[m], start=(t == 0 and m == 0), stop=(t == KD - 1 and m == 1))
                mm.then_inc(proj_done, 1)
                pe.wait_ge(pt_lo_made, val(pt_lo_made, l, 0))
                pe.wait_ge(*read_out(l, "ckv0"))
                pe.wait_ge(*read_out(l, "ckv1"))
                for b in range(TT):
                    pe.wait_ge(w_hi_made, val(w_hi_made, l, BLOCK_AT[("dv", b)] + 1))
                    pe.wait_ge(w_lo_made, val(w_lo_made, l, BLOCK_AT[("dv", b)] + 1))
                    s = SLOT[BLOCK_AT[("dv", b)]]
                    for tt in range(TT):
                        for k in range(2):
                            kk = 2 * b + k
                            mm = three(DV_BANKS[tt][:, :], [((u(kk)[0][:, tt * P:(tt + 1) * P],
                                                              u(kk)[1][:, tt * P:(tt + 1) * P]),
                                                             wtile(s, k, SEQ))], kk == 0, kk == KD - 1)
                    mm.then_inc(dv_done, 1)
                    if b == 0:
                        pe.wait_ge(ss_acc, val(ss_acc, l, KD + 2))
                        stat_c(l, MISC_AT["q_c"])
                    if b == 1:
                        stat_b(l, MISC_AT["q_b"], 1)
                    if b == 2:
                        pe.wait_ge(ss_acc, val(ss_acc, l, KD + 4))
                        stat_c(l, MISC_AT["kv_c"])
                    if b == 3:
                        stat_b(l, MISC_AT["kv_b"], 2)
                for use in FIRST_USES:
                    head_sum(l, use, range(KD))
                head_sum(l, SECOND_USES[0], range(KD))
                pe.wait_ge(dv_lo_made, val(dv_lo_made, l, TT))
                if l == 0:
                    pe.wait_ge(lam_m, 1)
                    nc.tensor.matmul(bank[7][:, 0:DEPTH], ones[0:4, :], lam_s[:, 2:2 + DEPTH], start=True, stop=True
                                     ).then_inc(lam_m, 1)
                scores_diff(l, 0, 0)
                scores_diff(l, 0, 1)
                scores_diff(l, 1, 0)
                scores_diff(l, 1, 1)
                head_sum(l, SECOND_USES[1], range(KD))
                for n in range(STEPS + 1):
                    if n + 2 < DSTEPS:
                        scores_diff(l, n + 2, 0)
                    elif n + 2 < STEPS:
                        scores(l, n + 2)
                    g, r = divmod(n - TT - 2, TT)
                    if r == 3 and 0 <= g < DIFF_HEADS:
                        stat_b(l, MISC_AT[f"sub{g}_b"], 3 + g)
                    for use, part in FILL.get(n, []):
                        if use[0] == "d":
                            head_sum(l, use, part)
                        elif use[0] == "o":
                            out_sum(l, use, part)
                        else:
                            if use == "q0":
                                pe.wait_ge(c_lo_made, val(c_lo_made, l, 2 * KC))
                            latent_sum(l, use)
                    if n >= STEPS - 1:
                        out_sum(l, OUTM_USES[n - STEPS + 1], range(0, 2))
                    if r == 0 and g >= 0:
                        values(l, g)
                    if n:
                        turn(l, n - 1)
                    if n + 2 < DSTEPS:
                        scores_diff(l, n + 2, 1)
                    if r == 1 and 0 <= g < DIFF_HEADS:
                        stat_c(l, MISC_AT[f"sub{g}_c"], tmp_s[:, 1, :])
                pe.wait_ge(sc_free, val(sc_free, l, 2 * DSTEPS + MSTEPS))
                for use in OUTM_USES[2:4]:
                    out_sum(l, use, range(0, 2))
                values(l, DIFF_HEADS + MLA_HEADS - 1)
                for use in OUTM_USES[:4]:
                    out_sum(l, use, range(2, TT - 1))
                for use in OUTM_USES[:4]:
                    out_sum(l, use, range(TT - 1, TT))
                for use in OUTM_USES[4:]:
                    out_sum(l, use, range(TT))
                def up_sum(l, c, i, part):
                    use = f"up{c}_{i}"
                    high, low = block_ready(l, BLOCK_AT[(f"up{c}", i)])
                    pe.wait_ge(*high)
                    pe.wait_ge(*low)
                    pe.wait_ge(*taken(l, use))
                    for k in part:
                        if c == 0:
                            pe.wait_ge(u_lo_made, val(u_lo_made, l, KD + k + 1))
                        mm = three(bank[BANK[use]][:, :], [(wtile(SLOT[BLOCK_AT[(f"up{c}", i)]], HALVES[k]), u(HALVES[k]))],
                                   k == 0, k == KD - 1)
                    if part[-1] == KD - 1:
                        mm.then_inc(proj_done, 1)

                for i in range(FC - 1):
                    up_sum(l, 0, i, range(0, KD // 2))
                for i in range(FC - 1):
                    up_sum(l, 0, i, range(KD // 2, KD))
                pe.wait_ge(ss_acc, val(ss_acc, l, 2 * KD + 2 * KC))
                stat_c(l, MISC_AT["mlp_c"])
                up_sum(l, 0, FC - 1, range(0, KD // 2))
                stat_b(l, MISC_AT["mlp_b"], 3 + DIFF_HEADS)
                up_sum(l, 0, FC - 1, range(KD // 2, KD))
                for kind, c in mlp_order()[1:]:
                    for i in range(FC):
                        if kind == "up":
                            up_sum(l, c, i, range(KD))
                            continue
                        key = (f"{kind}{c}", i)
                        s = SLOT[BLOCK_AT[key]]
                        pe.wait_ge(w_hi_made, val(w_hi_made, l, BLOCK_AT[key] + 1))
                        pe.wait_ge(w_lo_made, val(w_lo_made, l, BLOCK_AT[key] + 1))
                        for j in range(2):
                            use = f"down{c}_{2 * i + j}"
                            pe.wait_ge(*taken(l, use))
                            for t in range(FC):
                                if i == 0 and j == 0:
                                    pe.wait_ge(hid_lo_made, val(hid_lo_made, l, c * FC + t + 1))
                                w = tuple(x[:, s, t * 256 + j * P:t * 256 + (j + 1) * P] for x in (w_hi, w_lo))
                                mm = three(bank[BANK[use]][:, :], [(w, (hid_hi[:, c % 2, t, :], hid_lo[:, c % 2, t, :]))],
                                           t == 0, t == FC - 1)
                            mm.then_inc(proj_done, 1)
            for b in range(4):
                pe.wait_ge(bank_free[b], val(bank_free[b], DEPTH, 0))
            for j in range(KD // 2):
                pe.wait_ge(gh_made, j + 1)
                for tt in range(TT):
                    nc.tensor.transpose(Y_BANKS[0][tt][:, j * P:(j + 1) * P], gh[:, j, tt * P:(tt + 1) * P], ident[:, :])
            pe.wait_ge(ss_acc, val(ss_acc, DEPTH, KD))
            stat_c(DEPTH, 0)
            pe.wait_ge(misc_free, val(misc_free, DEPTH, 1))
            pe.wait_ge(gh_made, KD)
            for tt in range(TT):
                for j in range(KD // 2):
                    mm = nc.tensor.transpose(Y_BANKS[1][tt][:, j * P:(j + 1) * P],
                                             gh[:, KD // 2 + j, tt * P:(tt + 1) * P], ident[:, :])
                mm.then_inc(yt_done, 1)


OUT_SPLITS = dict(zip((21, 29, 37, 39, 41, 43, 45, 48), range(OUTD_AT, OUTM_AT + TT)))


_INS = ["x", "w_in", "g_mix", "g_q", "g_kv", "w_uq", "w_ukv", "lam_q1", "lam_k1", "lam_q2", "lam_k2",
        "g_sub", "w_out", "g_mlp", "w_up", "w_down", "g_final"]


def shape_constants(np):
    f = np.float32
    pos = np.arange(SEQ, dtype=f)
    inv = (f(1.0) / (f(ROPE_THETA) ** (np.arange(0, ROPE, 2, dtype=f) / f(ROPE)))).astype(f)
    ang = (pos[:, None] * inv[None, :]).astype(f)
    cos, sin = np.cos(ang).T, np.sin(ang).T
    c = np.zeros((P, C_W), f)
    scale = f(QK ** -0.5)
    c[0:NOPE, C_TABQ:C_TABQ + SEQ] = scale
    c[NOPE:QK, C_TABQ:C_TABQ + SEQ] = np.concatenate([cos, cos]) * scale
    c[QK:P, C_TABQ:C_TABQ + SEQ] = np.concatenate([-sin, sin]) * scale
    c[0:ROPE, C_TABK:C_TABK + SEQ] = np.concatenate([cos, cos])
    c[ROPE:2 * ROPE, C_TABK:C_TABK + SEQ] = np.concatenate([-sin, sin])
    c[:, C_NEGD:C_NEGD + NEGD] = -np.abs(np.arange(P)[:, None] + (TT - 1) * P - np.arange(NEGD)[None, :])
    for l in range(DEPTH):
        c[l, C_SIGN + l], c[DEPTH + l, C_SIGN + l] = 1.0, -1.0
        lam_init = 0.8 - 0.6 * math.exp(-0.3 * l)
        c[:, C_INIT + l] = lam_init
        c[:, C_GSC + l] = 1.0 - lam_init
    return c


def kernel(**inputs):
    import numpy as np
    import concourse.bacc as bacc
    from concourse.bass_utils import run_bass_kernel_spmd

    nc = bacc.Bacc("TRN2", target_bir_lowering=False, num_devices=1)
    arrays, args = {}, []
    for name in _INS:
        a = np.ascontiguousarray(inputs[name])
        arrays[f"in_{name}"] = a
        args.append(nc.dram_tensor(f"in_{name}", a.shape, mybir.dt.from_np(a.dtype), kind="ExternalInput").ap())
    c = shape_constants(np)
    arrays["in_cst"] = c
    args.append(nc.dram_tensor("in_cst", c.shape, F32, kind="ExternalInput").ap())
    args.append(nc.dram_tensor("out_0", (1, SEQ, D_MODEL), F32, kind="ExternalOutput").ap())
    trunk(nc, *args)
    r = run_bass_kernel_spmd(nc, [arrays], core_ids=[0])
    return r.results[0]["out_0"]
```
